# Optimizing a Trainium2 kernel written in Bass

```python
import math
import jax, jax.numpy as jnp
from jax import lax
import numpy as np

D_MODEL = 2048
BATCH = 1
SEQ = 128
DEPTH = 1
DEC_BATCH = 1
DEC_SEQ = 512
PAST_LEN = 128

GRID_W = 64
HEAD_DIM = 128
N_DIFF_HEADS = 8
DIFF_QK_DIM = HEAD_DIM // 2
N_GQA_HEADS = 8
N_GQA_KV_HEADS = 2
GQA_GROUP = N_GQA_HEADS // N_GQA_KV_HEADS
MIX_WIDTH = (N_DIFF_HEADS + N_GQA_HEADS) * HEAD_DIM
DIFF_QK_W = N_DIFF_HEADS * 2 * DIFF_QK_DIM
DIFF_V_W = N_DIFF_HEADS * HEAD_DIM
GQA_Q_W = N_GQA_HEADS * HEAD_DIM
GQA_KV_W = N_GQA_KV_HEADS * HEAD_DIM
IN_PROJ_W = 2 * DIFF_QK_W + DIFF_V_W + GQA_Q_W + 2 * GQA_KV_W
N_EXPERTS = 16
CAPACITY_FACTOR = 2
D_EXPERT = D_MODEL // 2
Q_BLOCK = 128
ROPE_THETA = 10000.0
NORM_EPS = 1e-6
N_MOD = 6

kernel_name = "hybrid_diff_gqa_ec_diffusion_step"

def lambda_init(layer_idx):
    return 0.8 - 0.6 * math.exp(-0.3 * layer_idx)

def rmsnorm(x, g):
    xf = x.astype(jnp.float32)
    y = xf * lax.rsqrt(jnp.mean(xf * xf, axis=-1, keepdims=True) + NORM_EPS)
    return (y * g.astype(jnp.float32)).astype(x.dtype)

def axial_rope_tables(n, dim, dtype):
    t = jnp.arange(n, dtype=jnp.int32)
    row = (t // GRID_W).astype(jnp.float32)
    col = (t % GRID_W).astype(jnp.float32)
    sec = dim // 2
    inv = ROPE_THETA ** (-jnp.arange(0, sec, 2, dtype=jnp.float32) / sec)
    ang = jnp.stack([row[:, None] * inv, col[:, None] * inv], axis=1)
    ang = jnp.concatenate([ang, ang], axis=-1).reshape(n, dim)
    return jnp.cos(ang).astype(dtype), jnp.sin(ang).astype(dtype)

def apply_rope(x, cos, sin):
    shp = x.shape
    dim = shp[-1]
    xs = x.reshape(shp[:-1] + (2, 2, dim // 4))
    rot = jnp.concatenate([-xs[..., 1:, :], xs[..., :1, :]], axis=-2).reshape(shp)
    bshape = (1, shp[1]) + (1,) * (x.ndim - 3) + (dim,)
    return x * cos.reshape(bshape) + rot * sin.reshape(bshape)

def _to_blocks(q):
    b, n = q.shape[:2]
    q = q.reshape((b, n // Q_BLOCK, Q_BLOCK) + q.shape[2:])
    return jnp.moveaxis(q, 1, 0)

def _from_blocks(o):
    o = jnp.moveaxis(o, 0, 1)
    return o.reshape((o.shape[0], -1) + o.shape[3:])

def diff_attention(q1, q2, k1, k2, v, lam):
    scale = DIFF_QK_DIM ** -0.5

    def block(qs):
        qb1, qb2 = qs
        a1 = jax.nn.softmax(jnp.einsum('bqhd,bkhd->bhqk', qb1, k1).astype(jnp.float32) * scale, axis=-1)
        a2 = jax.nn.softmax(jnp.einsum('bqhd,bkhd->bhqk', qb2, k2).astype(jnp.float32) * scale, axis=-1)
        a = (a1 - lam * a2).astype(v.dtype)
        return jnp.einsum('bhqk,bkhd->bqhd', a, v)

    return _from_blocks(lax.map(block, (_to_blocks(q1), _to_blocks(q2))))

def gqa_attention(q, k, v):
    b, n = q.shape[:2]
    scale = HEAD_DIM ** -0.5
    q = q.reshape(b, n, N_GQA_KV_HEADS, GQA_GROUP, HEAD_DIM)

    def block(qb):
        s = jnp.einsum('bqgrd,bkgd->bgrqk', qb, k).astype(jnp.float32) * scale
        p = jax.nn.softmax(s, axis=-1).astype(v.dtype)
        o = jnp.einsum('bgrqk,bkgd->bqgrd', p, v)
        return o.reshape(o.shape[0], o.shape[1], N_GQA_HEADS, HEAD_DIM)

    return _from_blocks(lax.map(block, _to_blocks(q)))

def ec_moe(h, w_router, w_gate, w_up, w_down):
    b, n, d = h.shape
    cap = CAPACITY_FACTOR * n // N_EXPERTS
    logits = jnp.einsum('bnd,de->bne', h, w_router).astype(jnp.float32)
    aff = jax.nn.softmax(logits, axis=-1)
    gate, idx = lax.top_k(jnp.swapaxes(aff, 1, 2), cap)
    xs = jax.vmap(lambda hb, ib: hb[ib])(h, idx)
    hid = jax.nn.silu(jnp.einsum('becd,edf->becf', xs, w_gate)) * jnp.einsum('becd,edf->becf', xs, w_up)
    out = jnp.einsum('becf,efd->becd', hid, w_down) * gate[..., None].astype(h.dtype)
    return jax.vmap(lambda ob, ib: jnp.zeros((n, d), h.dtype).at[ib.reshape(-1)].add(ob.reshape(-1, d)))(out, idx)

def trunk_layer(x, mod, rope, ctx_kv, lam_init, norm1_g, norm2_g, w_in, w_out, lq1, lk1, lq2, lk2,
                subln_g, qn_g, kn_g, w_router, w_gate, w_up, w_down):
    b, n, _ = x.shape
    sh1, sc1, g1, sh2, sc2, g2 = jnp.split(mod[:, None, :].astype(x.dtype), N_MOD, axis=-1)
    h = rmsnorm(x, norm1_g) * (1 + sc1) + sh1
    p = jnp.einsum('bnd,de->bne', h, w_in)
    splits = [DIFF_QK_W, 2 * DIFF_QK_W, 2 * DIFF_QK_W + DIFF_V_W, 2 * DIFF_QK_W + DIFF_V_W + GQA_Q_W,
              2 * DIFF_QK_W + DIFF_V_W + GQA_Q_W + GQA_KV_W]
    dq, dk, dv, gq, gk, gv = jnp.split(p, splits, axis=-1)
    dq = dq.reshape(b, n, N_DIFF_HEADS, 2, DIFF_QK_DIM)
    dk = dk.reshape(b, n, N_DIFF_HEADS, 2, DIFF_QK_DIM)
    dv = dv.reshape(b, n, N_DIFF_HEADS, HEAD_DIM)
    gq = rmsnorm(gq.reshape(b, n, N_GQA_HEADS, HEAD_DIM), qn_g)
    gk = rmsnorm(gk.reshape(b, n, N_GQA_KV_HEADS, HEAD_DIM), kn_g)
    gv = gv.reshape(b, n, N_GQA_KV_HEADS, HEAD_DIM)
    own_kv = (dk, dv, gk, gv)
    if rope is None:
        dk_all, dv_all, gk_all, gv_all = dk, dv, gk, gv
    else:
        dcos, dsin, gcos, gsin = rope
        dq = apply_rope(dq, dcos, dsin)
        gq = apply_rope(gq, gcos, gsin)
        ck_d, cv_d, ck_g, cv_g = ctx_kv
        dk_all = jnp.concatenate([ck_d.astype(x.dtype), apply_rope(dk, dcos, dsin)], axis=1)
        dv_all = jnp.concatenate([cv_d.astype(x.dtype), dv], axis=1)
        gk_all = jnp.concatenate([ck_g.astype(x.dtype), apply_rope(gk, gcos, gsin)], axis=1)
        gv_all = jnp.concatenate([cv_g.astype(x.dtype), gv], axis=1)
    lam = (jnp.exp(jnp.sum(lq1.astype(jnp.float32) * lk1.astype(jnp.float32)))
           - jnp.exp(jnp.sum(lq2.astype(jnp.float32) * lk2.astype(jnp.float32))) + lam_init)
    o_d = diff_attention(dq[..., 0, :], dq[..., 1, :], dk_all[..., 0, :], dk_all[..., 1, :], dv_all, lam)
    o_d = rmsnorm(o_d, subln_g) * (1.0 - lam_init)
    o_g = gqa_attention(gq, gk_all, gv_all)
    o = jnp.concatenate([o_d.reshape(b, n, DIFF_V_W), o_g.reshape(b, n, GQA_Q_W)], axis=-1)
    x = x + g1 * jnp.einsum('bne,ed->bnd', o, w_out)
    h2 = rmsnorm(x, norm2_g) * (1 + sc2) + sh2
    x = x + g2 * ec_moe(h2, w_router, w_gate, w_up, w_down)
    return x, own_kv

def setup_inputs(seed: int = 0) -> dict:
    key = jax.random.key(seed)
    ks = jax.random.split(key, 32)
    f32 = jnp.float32
    nrm = lambda k, shape, s: jax.random.normal(k, shape, f32) * s
    return {
        "x_prompt": nrm(ks[0], (BATCH, SEQ, D_MODEL), 1.0),
        "x_sample": nrm(ks[1], (DEC_BATCH, DEC_SEQ, D_MODEL), 1.0),
        "c": nrm(ks[2], (DEC_BATCH, D_MODEL), 1.0),
        "cache_diff_k": nrm(ks[3], (DEC_BATCH, DEPTH, PAST_LEN, N_DIFF_HEADS, 2, DIFF_QK_DIM), 1.0),
        "cache_diff_v": nrm(ks[4], (DEC_BATCH, DEPTH, PAST_LEN, N_DIFF_HEADS, HEAD_DIM), 1.0),
        "cache_gqa_k": nrm(ks[5], (DEC_BATCH, DEPTH, PAST_LEN, N_GQA_KV_HEADS, HEAD_DIM), 1.0),
        "cache_gqa_v": nrm(ks[6], (DEC_BATCH, DEPTH, PAST_LEN, N_GQA_KV_HEADS, HEAD_DIM), 1.0),
        "c_ctx": nrm(ks[7], (D_MODEL,), 1.0),
        "norm1_g": 1.0 + nrm(ks[8], (DEPTH, D_MODEL), 0.02),
        "norm2_g": 1.0 + nrm(ks[9], (DEPTH, D_MODEL), 0.02),
        "w_mod": nrm(ks[10], (DEPTH, D_MODEL, N_MOD * D_MODEL), 0.5 * D_MODEL ** -0.5),
        "b_mod": nrm(ks[11], (DEPTH, N_MOD * D_MODEL), 0.02),
        "w_in": nrm(ks[12], (DEPTH, D_MODEL, IN_PROJ_W), D_MODEL ** -0.5),
        "w_out": nrm(ks[13], (DEPTH, MIX_WIDTH, D_MODEL), MIX_WIDTH ** -0.5),
        "diff_lambda_q1": nrm(ks[14], (DEPTH, DIFF_QK_DIM), 0.1),
        "diff_lambda_k1": nrm(ks[15], (DEPTH, DIFF_QK_DIM), 0.1),
        "diff_lambda_q2": nrm(ks[16], (DEPTH, DIFF_QK_DIM), 0.1),
        "diff_lambda_k2": nrm(ks[17], (DEPTH, DIFF_QK_DIM), 0.1),
        "diff_subln_g": 1.0 + nrm(ks[18], (DEPTH, HEAD_DIM), 0.02),
        "gqa_q_norm_g": 1.0 + nrm(ks[19], (DEPTH, HEAD_DIM), 0.02),
        "gqa_k_norm_g": 1.0 + nrm(ks[20], (DEPTH, HEAD_DIM), 0.02),
        "w_router": nrm(ks[21], (DEPTH, D_MODEL, N_EXPERTS), D_MODEL ** -0.5),
        "w_expert_gate": nrm(ks[22], (DEPTH, N_EXPERTS, D_MODEL, D_EXPERT), D_MODEL ** -0.5),
        "w_expert_up": nrm(ks[23], (DEPTH, N_EXPERTS, D_MODEL, D_EXPERT), D_MODEL ** -0.5),
        "w_expert_down": nrm(ks[24], (DEPTH, N_EXPERTS, D_EXPERT, D_MODEL), D_EXPERT ** -0.5),
        "final_norm_g": 1.0 + nrm(ks[25], (D_MODEL,), 0.02),
    }

def reference(x_prompt, x_sample, c, cache_diff_k, cache_diff_v, cache_gqa_k, cache_gqa_v, c_ctx,
              norm1_g, norm2_g, w_mod, b_mod, w_in, w_out, diff_lambda_q1, diff_lambda_k1,
              diff_lambda_q2, diff_lambda_k2, diff_subln_g, gqa_q_norm_g, gqa_k_norm_g, w_router,
              w_expert_gate, w_expert_up, w_expert_down, final_norm_g):
    n_lat = x_sample.shape[1]
    dcos, dsin = axial_rope_tables(n_lat, DIFF_QK_DIM, x_sample.dtype)
    gcos, gsin = axial_rope_tables(n_lat, HEAD_DIM, x_sample.dtype)
    rope = (dcos, dsin, gcos, gsin)
    c_ctx_b = jnp.broadcast_to(c_ctx[None, :], (x_prompt.shape[0], D_MODEL))
    xp, xs = x_prompt, x_sample
    new_dk, new_dv, new_gk, new_gv = [], [], [], []
    for l in range(DEPTH):
        lam_init = lambda_init(l)
        lw = (norm1_g[l], norm2_g[l], w_in[l], w_out[l], diff_lambda_q1[l], diff_lambda_k1[l],
              diff_lambda_q2[l], diff_lambda_k2[l], diff_subln_g[l], gqa_q_norm_g[l], gqa_k_norm_g[l],
              w_router[l], w_expert_gate[l], w_expert_up[l], w_expert_down[l])
        mod_ctx = jnp.einsum('bd,de->be', jax.nn.silu(c_ctx_b), w_mod[l]) + b_mod[l]
        mod_lat = jnp.einsum('bd,de->be', jax.nn.silu(c), w_mod[l]) + b_mod[l]
        xp, (dk, dv, gk, gv) = trunk_layer(xp, mod_ctx, None, None, lam_init, *lw)
        new_dk.append(dk)
        new_dv.append(dv)
        new_gk.append(gk)
        new_gv.append(gv)
        ctx_kv = (cache_diff_k[:, l], cache_diff_v[:, l], cache_gqa_k[:, l], cache_gqa_v[:, l])
        xs, _ = trunk_layer(xs, mod_lat, rope, ctx_kv, lam_init, *lw)
    y_prompt = rmsnorm(xp, final_norm_g)
    y_sample = rmsnorm(xs, final_norm_g)
    return (y_prompt, y_sample, jnp.stack(new_dk, axis=1), jnp.stack(new_dv, axis=1),
            jnp.stack(new_gk, axis=1), jnp.stack(new_gv, axis=1))


_drawn_inputs = setup_inputs


def setup_inputs(seed=0):
    import zlib

    import numpy as np

    out = dict(_drawn_inputs(seed))
    spreads = {}
    factors = {'cache_gqa_k': 8.0,
     'cache_gqa_v': 7.903,
     'norm1_g': 2.94,
     'norm2_g': 8.0,
     'diff_lambda_q1': 8.0,
     'diff_lambda_k1': 4.031,
     'diff_lambda_q2': 3.84,
     'diff_subln_g': 8.0,
     'gqa_q_norm_g': 8.0,
     'gqa_k_norm_g': 2.973,
     'final_norm_g': 7.308,
     'cache_diff_k': 8.0,
     'cache_diff_v': 8.0}
    for name, (base, spread) in spreads.items():
        noise = np.random.default_rng([zlib.crc32(name.encode()), seed]).standard_normal(out[name].shape)
        drawn = base * np.exp(spread * noise) if base else spread * noise
        out[name] = __import__('jax').numpy.asarray(drawn.astype(out[name].dtype))
    for name, factor in factors.items():
        out[name] = (out[name] * factor).astype(out[name].dtype)
    return out
```

```python
import math
from contextlib import ExitStack

import numpy as np

import concourse.bass as bass
from concourse import mybir
from concourse.alu_op_type import AluOpType as ALU

F32 = mybir.dt.float32
BF16 = mybir.dt.bfloat16
U32 = mybir.dt.uint32
ACT = mybir.ActivationFunctionType
AX = mybir.AxisListType.X

P = 128
D = 2048
KC = D // P
LAT, CTX = 512, 128
TOK = LAT + CTX
NT = TOK // P
TL = LAT // P
PAST = 128
NB = 512
HD = 128
DH, GH, KVH = 8, 8, 2
HEADS = DH + GH
GRP = GH // KVH
PROJ = 4608
VW = DH * HD + KVH * HD
NE = 16
DE = 1024
CL, CX = 2 * LAT // NE, 2 * CTX // NE
CAP = CL + CX
EPS = 1e-6
LAM_INIT = 0.8 - 0.6 * math.exp(-0.3 * 0)
GRID_W = 64
DQ = HD // 2
SLOT = 2048
RING_B = 4
RING_E = 12
XCH = 24
ORDER = [8, 6, 7, 2, 3, 4, 0, 1, 5]
ROWS_BLOCKS = [b for b in ORDER if b not in (4, 5)]
KEY_BLOCKS = (8, 2, 3)
MOD_PACE = [(2, 2, 3, 3), (1, 3, 3, 3), (0, 2, 3, 3), (0, 2, 3, 3), (1, 3, 3, 3), (1, 3, 3, 3), (2, 2, 2, 2)]
assert sum(map(sum, MOD_PACE)) == 4 * KC
UNITS = NT * HEADS


def tensor_steps():
    steps = [("vectors",), ("bmod",)]
    steps += [("modA", m, k) for m in range(2) for k in range(KC)]
    steps += [("cols", 0), ("cols", 1), ("x", 0)]
    late = [("modB", m, k) for m in range(2, 6) for k in range(KC)]
    sums = []
    for p, b in enumerate(ORDER):
        for q in range(4):
            pace = MOD_PACE[p][q] if p < len(MOD_PACE) else 0
            for j in range(4):
                k = 4 * q + j
                if p == 0 and k + 1 < KC:
                    steps.append(("x", k + 1))
                steps.append(("projk", b, k))
                steps += sums
                sums = []
                if j >= 4 - pace:
                    steps.append(late.pop(0))
                    if steps[-1][2] == KC - 1:
                        sums = [("sum", steps[-1][1])]
            if p > 0 and ORDER[p - 1] in ROWS_BLOCKS:
                steps += [("rows", ORDER[p - 1], t) for t in ([q] if q < 3 else [3, 4])]
            if p == 1 and q == 0:
                steps += [("cache", i) for i in range(3)]
    return steps + [("cols2",)]


STEPS = tensor_steps()


def plan_loads():
    proj = [("proj", b, q) for b in ORDER for q in range(4)]
    beside, j = {}, -1
    for s in STEPS:
        if s[0] == "projk" and s[2] % 4 == 0:
            j += 1
        if s[0] == "modB":
            beside.setdefault(j, []).append(s)
    order = [s for s in STEPS if s[0] == "modA"] + [proj[0]]
    for j in range(len(proj)):
        order += proj[j + 1:j + 2] + beside.get(j, [])
    order += [("out", n, q) for n in range(4) for q in range(4)]
    counts = {"modA": 0, "proj": 0, "modB": 0, "out": 0}
    tensor = {"modA": 0, "proj": 2 * KC, "out": 2 * KC + len(proj)}
    fills, last, plan = [0] * RING_B, [None] * RING_B, {}
    for c in order:
        kind, n = c[0], counts[c[0]]
        counts[kind] += 1
        slot = {"modA": n % 4, "proj": n % 2, "modB": 2 + n % 2, "out": n % 4}[kind]
        before = last[slot]
        fills[slot] += 1
        last[slot] = ("vector", n + 1) if kind == "modB" else ("tensor", tensor[kind] + n + 1)
        plan[c] = (slot, fills[slot], before)
    return order, plan, last


LOADS, PLAN, LAST_USE = plan_loads()
XP = [s for s in STEPS if s[0] in ("vectors", "bmod", "cache", "x", "rows", "cols", "cols2")]


def transposes_before(step):
    n = 0
    for s in XP:
        if s == step:
            return n
        n += 2 if s[0] == "x" else 1


XP_TOTAL = sum(2 if s[0] == "x" else 1 for s in XP)
ROPED = [(b, t) for b in ROWS_BLOCKS for t in range(NT) if b >= 6 or t < TL]


def proj_count(b, t):
    return ORDER.index(b) * NT + t + 1


def build(nc, a, rope, outs):
    (x_prompt, x_sample, cvec, cache_dk, cache_dv, cache_gk, cache_gv, c_ctx, norm1_g, norm2_g, w_mod, b_mod,
     w_in, w_out, lq1, lk1, lq2, lk2, subln_g, qn_g, kn_g, w_router, w_gate, w_up, w_down, final_g) = a
    y_prompt, y_sample, new_dk, new_dv, new_gk, new_gv = outs

    ctx = ExitStack()
    with ctx:
        def sb(name, shape, dt=F32):
            return ctx.enter_context(nc.sbuf_tensor(name, shape, dt))

        def sem(name):
            return ctx.enter_context(nc.semaphore(name))

        acc_d = nc.dram_tensor("acc_d", [TOK, D], F32, kind="Internal").ap()
        xn_d = nc.dram_tensor("xn_d", [TOK, D], F32, kind="Internal").ap()
        mod_d = nc.dram_tensor("mod_d", [4, 2, D], F32, kind="Internal").ap()

        H0 = 0
        R0 = H0 + KC * TOK
        Q0 = R0 + RING_B * SLOT
        K0 = Q0 + HEADS * TOK
        V0 = K0 + (DH + KVH) * (TOK + PAST)
        S0 = V0 + (NT + 1) * VW
        X0 = R0 + RING_E * SLOT
        W0 = X0 + NT * D
        END = S0 + 7040
        assert S0 >= X0 and END - W0 >= 5632
        arena = sb("arena", [P, END])

        def at(off, *dims):
            v = arena[:, off:off + int(np.prod(dims))]
            if len(dims) == 2:
                v = v.rearrange("p (a b) -> p a b", a=dims[0])
            elif len(dims) == 3:
                v = v.rearrange("p (a b c) -> p a b c", a=dims[0], b=dims[1])
            elif len(dims) == 4:
                v = v.rearrange("p (a b c d) -> p a b c d", a=dims[0], b=dims[1], c=dims[2])
            return v

        hT = at(H0, KC, TOK)
        oT = at(H0, HEADS, TOK)
        xrows = at(K0, NT, D)
        mrowA = at(Q0, 2, D)[0:2]
        macc = at(Q0, 2, D)
        cdk_rows = at(Q0 + 4096, DH * HD)
        cgk_rows = at(Q0 + 4096 + DH * HD, KVH * HD)
        vrows = at(Q0 + 5376, P)[0:65, :]
        brows = at(Q0 + 5504, P)[0:96, :]
        lamv = at(Q0 + 5632, 2, 2, DQ)
        junkA = at(Q0 + 8192, D)
        qT = at(Q0, HEADS, TOK)
        kT = at(K0, DH + KVH, TOK + PAST)
        V = at(V0, NT + 1, VW)
        ropeD = at(S0, TL, 2, DQ)
        ropeQ = at(S0 + 512, TL, 2, HD)
        ropeK = at(S0 + 1536, TL, 2, HD)
        prow = at(S0 + 2560, NT, NB)
        ry = at(S0 + 5120, NB)
        rz = at(S0 + 5632, NB)
        E = at(S0, 2, 2, TOK)
        PT = at(S0 + 2560, 2, TOK)
        orow = at(S0 + 3840, HEADS, HD)
        osq = at(S0 + 5888, DH * HD)
        x1 = at(X0, NT, D)
        G1 = at(W0, 2, D)
        gtmp = at(W0 + 4096, NB)
        junkD = at(W0 + 4608, NB // 2).bitcast(BF16)
        wr = at(W0 + 4864, KC, NE)
        wrm = at(W0 + 5120, 2, KC, NE)
        x1T = sb("x1T", [P, 2, 4 * P])
        xn = at(H0, NT, D)
        xs = at(H0, D)
        xsT = at(H0 + 2048, KC, CAP)
        xstage = at(H0 + 3328, KC, CAP)
        sg = at(H0 + 4608, DE)
        hid = at(H0 + 5632, DE)
        hidT = at(H0 + 6656, DE // P, CAP)
        xrow_out = at(H0 + 7296, D)
        G2 = at(W0 + 2048, D)
        fgB = at(W0, D)
        junkF = at(R0, D)

        ident = sb("ident", [P, P])
        vecT = sb("vecT", [P, 65])
        bmodT = sb("bmodT", [P, 96])
        cT = sb("cT", [P, KC, 2])
        ctmp = sb("ctmp", [P, 32])
        modT = sb("modT", [P, 6, 2, KC])
        A1 = sb("A1", [P, 2, KC])
        A2 = sb("A2", [P, 2, KC])
        colrows = at(S0 + 6400, P)[0:64, :]
        mstage = at(S0 + 6528, NB)
        selv = sb("selv", [P, 2, 32])
        gains = at(S0 + 6144, 2, HD)
        lams = sb("lams", [P, 2])
        lame = sb("lame", [P, 2])
        neglam = sb("neglam", [P, 1])
        mhalf = sb("mhalf", [P, 8])
        ssx = sb("ssx", [P, NT])
        rstd = sb("rstd", [P, NT])
        ssg = sb("ssg", [P, 4])
        rg = sb("rg", [P, 4])
        mx = sb("mx", [P, 2])
        nmax = sb("nmax", [P, 4, 2])
        ssum = sb("ssum", [P, 4, 2])
        rsum = sb("rsum", [P, 4, 2])
        coef = sb("coef", [P, 1])
        sso = sb("sso", [P, DH])
        ro = sb("ro", [P, DH])
        ss2 = sb("ss2", [P, NT, 4])
        ms2 = sb("ms2", [P, NT])
        rstd2 = sb("rstd2", [P, NT])
        sel = at(W0 + 1024, 2, P)[0:2]
        cst = sb("cst", [2, NE])
        cstB = sb("cstB", [P, 2, NE])
        logit = at(W0 + 5632, NT, NE)
        aff = at(W0 + 5632 + NT * NE, NT, NE)
        lmax = sb("lmax", [P, NT])
        affT = at(W0, TOK)[0:NE, :]
        vals = at(W0 + TOK, CAP)[0:NE, :]
        idx = at(W0 + TOK + CAP, CAP)[0:NE, :].bitcast(U32)
        idxf = at(W0 + TOK + 2 * CAP, CAP)[0:NE, :]
        gateC = sb("gateC", [CAP, NE])
        idxC = sb("idxC", [CAP, NE], U32)
        gcol = sb("gcol", [CAP, 1])
        idxg = sb("idxg", [CAP, 1], U32)
        idxs = sb("idxs", [CAP, 1], U32)
        ssf = sb("ssf", [P, NT])
        rf = sb("rf", [P, NT])
        flag = sb("flag", [P, 1])

        ps = ctx.enter_context(nc.psum_tensor("ps", [P, 8 * 512], F32))

        def bank(i, n=1):
            return ps[:, 512 * i:512 * (i + n)]

        landed = [sem(f"landed{i}") for i in range(RING_B)]
        used = sem("used")
        mod_used = sem("mod_used")
        xlanded = [sem(f"xlanded{i}") for i in range(RING_E)]
        xused = sem("xused")
        x_in = [sem(f"x_in{t}") for t in range(NT)]
        small_in = sem("small_in")
        rope_in = sem("rope_in")
        cache_in = sem("cache_in")
        v_in = sem("v_in")
        ident_half = sem("ident_half")
        ident_ready = sem("ident_ready")
        const_ready = sem("const_ready")
        dve_step = sem("dve_step")
        x_squared = sem("x_squared")
        ms_ready = sem("ms_ready")
        rstd_ready = sem("rstd_ready")
        xn_ready = sem("xn_ready")
        silu_exp = sem("silu_exp")
        lam_sum = sem("lam_sum")
        lam_exp = sem("lam_exp")
        c_ready = sem("c_ready")
        xp_done = sem("xp_done")
        xp_taken = sem("xp_taken")
        modA_done = sem("modA_done")
        modA_act = sem("modA_act")
        modA_dve = sem("modA_dve")
        modT_ready = sem("modT_ready")
        selv_zero = sem("selv_zero")
        selv_ready = sem("selv_ready")
        bias_in = sem("bias_in")
        sum_done = sem("sum_done")
        sum_taken = sem("sum_taken")
        mod_stored = sem("mod_stored")
        colrows_in = sem("colrows_in")
        proj_done = sem("proj_done")
        proj_taken = sem("proj_taken")
        rowms_ready = sem("rowms_ready")
        rowr_ready = sem("rowr_ready")
        roped = sem("roped")
        k_out = sem("k_out")
        v_out = sem("v_out")
        gk_normed = sem("gk_normed")
        g1_in = sem("g1_in")
        scored = sem("scored")
        tail_scored = sem("tail_scored")
        max_done = sem("max_done")
        exp_done = sem("exp_done")
        probs_ready = sem("probs_ready")
        pt_done = sem("pt_done")
        pt_act = sem("pt_act")
        pt_dve = sem("pt_dve")
        av_done = sem("av_done")
        o_taken = sem("o_taken")
        oms_ready = sem("oms_ready")
        or_ready = sem("or_ready")
        onorm_ready = sem("onorm_ready")
        ot_done = sem("ot_done")
        ot_taken = sem("ot_taken")
        x_again = [sem(f"x_again{t}") for t in range(NT)]
        out_done = sem("out_done")
        out_taken = sem("out_taken")
        x1_done = sem("x1_done")
        x1_squared = sem("x1_squared")
        rt_done = sem("rt_done")
        rt_taken = sem("rt_taken")
        logits_done = sem("logits_done")
        router_w = sem("router_w")
        wr_in = sem("wr_in")
        sel_ready = sem("sel_ready")
        cst_done = sem("cst_done")
        cst_taken = sem("cst_taken")
        ms2_ready = sem("ms2_ready")
        rstd2_ready = sem("rstd2_ready")
        lshift_ready = sem("lshift_ready")
        lexp_done = sem("lexp_done")
        aff_ready = sem("aff_ready")
        affT_done = sem("affT_done")
        topk_ready = sem("topk_ready")
        cols_done = sem("cols_done")
        cols_ready = sem("cols_ready")
        xn2_ready = sem("xn2_ready")
        xn_stored = [sem(f"xn_stored{t}") for t in range(NT)]
        acc_stored = sem("acc_stored")
        fg_in = sem("fg_in")
        g2_in = sem("g2_in")
        idx_set = sem("idx_set")
        gathered = sem("gathered")
        t1_done = sem("t1_done")
        t1_scaled = sem("t1_scaled")
        xsT_ready = sem("xsT_ready")
        sig_exp = sem("sig_exp")
        sig_add = sem("sig_add")
        sig_rec = sem("sig_rec")
        sig_mul = sem("sig_mul")
        hid_half = sem("hid_half")
        ht_done = sem("ht_done")
        hidT_half = sem("hidT_half")
        gcol_ready = sem("gcol_ready")
        rows_ready = sem("rows_ready")
        scattered = sem("scattered")
        row_free = sem("row_free")
        xs_ready = sem("xs_ready")
        acc_in = [sem(f"acc_in{t}") for t in range(NT)]
        f_squared = sem("f_squared")
        fms_ready = sem("fms_ready")
        frstd_ready = sem("frstd_ready")
        y_ready = sem("y_ready")
        y_out = sem("y_out")

        N_SMALL = 12

        w_mod_v = w_mod.rearrange("o (k p) n -> (o k) p n", p=P)
        w_in_v = w_in.rearrange("o (q j p) n -> (o q) p j n", j=4, p=P)
        w_out_v = w_out.rearrange("o (q j p) n -> (o q) p j n", j=4, p=P)
        wg_v = w_gate.rearrange("o e (j i p) n -> (o e) j p i n", i=2, p=P)
        wu_v = w_up.rearrange("o e (j i p) n -> (o e) j p i n", i=2, p=P)
        wd_v = w_down.rearrange("o e (f p) n -> (o e) f p n", p=P)

        def slot_b(c):
            return R0 + PLAN[c][0] * SLOT

        def slot_e(j):
            return R0 + (j % RING_E) * SLOT

        def x_dram(t):
            return x_sample[0, P * t:P * (t + 1), :] if t < TL else x_prompt[0]

        def unit(u):
            t, j = u // HEADS, u % HEADS
            nc_, keys = (2 if j < DH else 1), (LAT + PAST if t < TL else CTX)
            kh = j if j < DH else DH + (j - DH) // GRP
            scale = (DQ if j < DH else HD) ** -0.5
            return t, j, nc_, keys, kh, scale

        def is_diff(u):
            return u % HEADS < DH

        def diff_before(u):
            return (u // HEADS) * DH + min(u % HEADS, DH)

        def pt_copied(eng, u):
            if is_diff(u):
                eng.wait_ge(pt_act, diff_before(u + 1))
            else:
                eng.wait_ge(pt_dve, u + 1 - diff_before(u + 1))

        def ot_round(u):
            t, j = u // HEADS, u % HEADS
            if j in (11, 13):
                return t, (j - 11) // 2
            if j in (1, 3) and t > 0:
                return t - 1, 2 + (j - 1) // 2
            return None

        OT_LIST = [ot_round(u) for u in range(UNITS) if ot_round(u)] + [(NT - 1, 2), (NT - 1, 3)]

        def S_ps(u):
            return bank(3 * (u % 2), 3)

        block = ctx.enter_context(nc.Block())

        @block.sync
        def _(sp):
            def chunk_b(c):
                slot, _, before = PLAN[c]
                if before:
                    sp.wait_ge(mod_used if before[0] == "vector" else used, before[1])
                if c[0] in ("modA", "modB"):
                    sp.dma_start(at(slot_b(c), D), w_mod_v[c[2], :, c[1] * D:(c[1] + 1) * D]).then_inc(landed[slot], 16)
                else:
                    src = w_in_v if c[0] == "proj" else w_out_v
                    sp.dma_start(at(slot_b(c), 4, NB), src[c[2], :, :, c[1] * NB:(c[1] + 1) * NB])\
                        .then_inc(landed[slot], 16)

            def chunk_e(e, j):
                s = slot_e(j)
                if j < 16:
                    w = wg_v if j < 8 else wu_v
                    src = w[bass.ds(e, 1), j % 8].rearrange("e p i n -> (e p) i n")
                    sp.dma_start(at(s, 2, DE), src).then_inc(xlanded[j % RING_E], 16)
                else:
                    src = wd_v[bass.ds(e, 1), j - 16].rearrange("e p n -> (e p) n")
                    sp.dma_start(at(s, D), src).then_inc(xlanded[j % RING_E], 16)

            for c in LOADS:
                chunk_b(c)
            sp.wait_ge(av_done, UNITS)
            sp.wait_ge(v_out, 32)
            for j in range(RING_B, RING_E):
                chunk_e(0, j)
            for j in range(RING_B):
                sp.wait_ge(used, LAST_USE[j][1])
                chunk_e(0, j)
            for j in range(RING_E, XCH):
                sp.wait_ge(xused, j - RING_E + 1)
                chunk_e(0, j)
            with sp.Fori(1, NE) as e:
                for j in range(XCH):
                    sp.wait_ge(xused, e * XCH + (j - RING_E + 1))
                    chunk_e(e, j)
            sp.wait_ge(y_out, 16 * NT)

        @block.tensor
        def _(pe):
            def ring_wait(c):
                pe.wait_ge(landed[PLAN[c][0]], 16 * PLAN[c][1])

            def xp_bank(i):
                if i >= 2:
                    pe.wait_ge(xp_taken, i - 1)
                return bank(6 + i % 2)

            pe.wait_ge(ident_ready, 1)
            for step in STEPS:
                kind = step[0]
                if kind == "vectors":
                    pe.wait_ge(small_in, 16 * N_SMALL)
                    b = xp_bank(transposes_before(step))
                    pe.transpose(b[:, 0:65], vrows[:, :], ident[0:65, 0:65]).then_inc(xp_done, 1)
                elif kind == "bmod":
                    b = xp_bank(transposes_before(step))
                    pe.transpose(b[:, 0:96], brows[:, :], ident[0:96, 0:96]).then_inc(xp_done, 1)
                elif kind == "cache":
                    b = xp_bank(transposes_before(step))
                    if step[1] == 0:
                        pe.wait_ge(cache_in, 32)
                    for h in range(4 if step[1] < 2 else 2):
                        src = cdk_rows[:, HD * (4 * step[1] + h):HD * (4 * step[1] + h + 1)] if step[1] < 2 \
                            else cgk_rows[:, HD * h:HD * (h + 1)]
                        mm = pe.transpose(b[:, HD * h:HD * (h + 1)], src, ident[:, :])
                    mm.then_inc(xp_done, 1)
                elif kind == "cols":
                    m = step[1]
                    pe.wait_ge(modA_act, m + 1)
                    if m == 0:
                        pe.wait_ge(modA_act, 2)
                        pe.wait_ge(modA_dve, 1)
                    b = xp_bank(transposes_before(step))
                    for k in range(KC):
                        mm = pe.transpose(b[:, 2 * k:2 * k + 2], mrowA[:, m, P * k:P * (k + 1)], ident[0:2, 0:2])
                    mm.then_inc(xp_done, 1)
                elif kind == "cols2":
                    pe.wait_ge(colrows_in, 64)
                    b = xp_bank(transposes_before(step))
                    pe.transpose(b[:, 0:64], colrows[:, :], ident[0:64, 0:64]).then_inc(xp_done, 1)
                elif kind == "sum":
                    m = step[1]
                    if m == 2:
                        pe.wait_ge(selv_ready, 2)
                    else:
                        pe.wait_ge(sum_taken, m - 2)
                    pe.wait_ge(mod_used, (m - 1) * KC)
                    for r in range(4):
                        for v in range(2):
                            mm = pe.matmul(bank(5)[32 * r:32 * (r + 1), :], selv[:, v, :], macc[:, v, NB * r:NB * (r + 1)],
                                           start=(v == 0), stop=(v == 1), skip_group_check=True)
                    mm.then_inc(sum_done, 1)
                elif kind == "x":
                    k = step[1]
                    if k == 0:
                        pe.wait_ge(xn_ready, NT)
                    i = transposes_before(step)
                    b = xp_bank(i)
                    for t in range(TL):
                        mm = pe.transpose(b[:, P * t:P * (t + 1)], xrows[:, t, P * k:P * (k + 1)], ident[:, :])
                    mm.then_inc(xp_done, 1)
                    b = xp_bank(i + 1)
                    pe.transpose(b[:, 0:P], xrows[:, TL, P * k:P * (k + 1)], ident[:, :]).then_inc(xp_done, 1)
                elif kind == "modA":
                    _, m, k = step
                    if k == 0:
                        if m == 0:
                            pe.wait_ge(c_ready, 1)
                        else:
                            pe.wait_ge(xp_taken, 2)
                    ring_wait(step)
                    w = at(slot_b(step), 4, NB)
                    for c in range(4):
                        mm = pe.matmul(bank(4 * m + c)[0:2, :], cT[:, k, :], w[:, c, :], start=(k == 0), stop=(k == KC - 1))
                    if k < KC - 1:
                        mm.then_inc(used, 1)
                    else:
                        mm.then_inc(modA_done, 1)
                        pe.wait_ge(modA_done, m + 1)
                        pe.sem_inc(used, 1)
                elif kind == "projk":
                    _, blk, k = step
                    c = ("proj", blk, k // 4)
                    o = ORDER.index(blk)
                    if k % 4 == 0:
                        ring_wait(c)
                    if o == 0:
                        pe.wait_ge(xp_taken, transposes_before(("x", k)) + 2)
                    if k == 0 and o == 0:
                        pe.wait_ge(modA_act, 2)
                    w = at(slot_b(c), 4, NB)
                    for t in range(NT):
                        if k == 0 and o > 0:
                            pe.wait_ge(proj_taken, NT * (o - 1) + t + 1)
                        mm = pe.matmul(bank(t), hT[:, k, P * t:P * (t + 1)], w[:, k % 4, :],
                                       start=(k == 0), stop=(k == KC - 1))
                        if k == KC - 1 and t < NT - 1:
                            mm.then_inc(proj_done, 1)
                    if k == KC - 1:
                        mm.then_inc(proj_done, 1)
                        pe.wait_ge(proj_done, NT * (o + 1))
                        pe.sem_inc(used, 1)
                    elif k % 4 == 3:
                        mm.then_inc(used, 1)
                elif kind == "rows":
                    _, blk, t = step
                    b = xp_bank(transposes_before(step))
                    if (blk, t) in ROPED:
                        pe.wait_ge(roped, ROPED.index((blk, t)) + 1)
                    else:
                        pe.wait_ge(proj_taken, proj_count(blk, t))
                    for h in range(2 if blk == 8 else 4):
                        mm = pe.transpose(b[:, HD * h:HD * (h + 1)], prow[:, t, HD * h:HD * (h + 1)], ident[:, :])
                    mm.then_inc(xp_done, 1)

            def scores(u):
                t, j, comps, keys, kh, _ = unit(u)
                S = S_ps(u)
                k0 = 0 if t < TL else LAT + PAST
                if u >= 2:
                    pe.wait_ge(exp_done, u - 1)
                qs = slice(P * t, P * (t + 1))
                if comps == 1:
                    parts = [(0, 0, LAT), (0, LAT, keys)] if t < TL else [(0, 0, keys)]
                elif t < TL:
                    parts = [(0, LAT, keys), (1, 384, keys), (0, 0, LAT), (1, 0, 384)]
                else:
                    parts = [(0, 0, keys), (1, 0, keys)]
                for n, (c, lo, hi) in enumerate(parts):
                    if n == 3:
                        pe.wait_ge(tail_scored, diff_before(u + 1))
                    rows = slice(0, HD) if comps == 1 else slice(DQ * c, DQ * (c + 1))
                    mm = pe.matmul(S[:, TOK * c + lo:TOK * c + hi], qT[rows, j, qs], kT[rows, kh, k0 + lo:k0 + hi],
                                   start=True, stop=True, skip_group_check=True)
                    if n == 0 and len(parts) == 4:
                        mm.then_inc(tail_scored, 1)
                mm.then_inc(scored, 1)

            def prob_transposes(u):
                t, j, comps, keys, _, _ = unit(u)
                pe.wait_ge(probs_ready, u + 1)
                if not is_diff(u):
                    pe.wait_ge(exp_done, u + 1)
                if u >= 1:
                    pt_copied(pe, u - 1)
                n_ot = len([v for v in range(u) if ot_round(v)])
                if n_ot:
                    pe.wait_ge(ot_taken, n_ot)
                for b in range(min(4, keys // P)):
                    mm = pe.transpose(bank(6)[:, P * b:P * (b + 1)], E[:, u % 2, 0, P * b:P * (b + 1)], ident[:, :])
                if keys > 4 * P:
                    if u >= 1:
                        pe.wait_ge(o_taken, u)
                    mm = pe.transpose(bank(7)[:, 0:P], E[:, u % 2, 0, 4 * P:5 * P], ident[:, :])
                mm.then_inc(pt_done, 1)

            def values(u):
                t, j, comps, keys, kh, _ = unit(u)
                pt_copied(pe, u)
                if u >= 1:
                    pe.wait_ge(o_taken, u)
                col = HD * kh
                nb = keys // P
                for b in range(nb):
                    mm = pe.matmul(bank(7)[:, P:2 * P], PT[:, u % 2, P * b:P * (b + 1)],
                                   V[:, b if t < TL else NT, col:col + HD], start=(b == 0), stop=(b == nb - 1))
                mm.then_inc(av_done, 1)

            def out_transposes(t, r):
                if r < 2:
                    pe.wait_ge(onorm_ready, t + 1)
                else:
                    pe.wait_ge(o_taken, HEADS * t + DH + 4 * (r - 2) + 4)
                for h in range(4):
                    mm = pe.transpose(bank(6)[:, HD * h:HD * (h + 1)], orow[:, 4 * r + h, :], ident[:, :])
                mm.then_inc(ot_done, 1)

            pe.wait_ge(xp_taken, XP_TOTAL)
            pe.wait_ge(proj_taken, NT * len(ORDER))
            pe.wait_ge(sum_taken, 4)
            pe.wait_ge(v_in, 32)
            scores(0)
            scores(1)
            for u in range(UNITS):
                prob_transposes(u)
                if u + 2 < UNITS:
                    scores(u + 2)
                values(u)
                if ot_round(u):
                    pt_copied(pe, u)
                    out_transposes(*ot_round(u))
            out_transposes(NT - 1, 2)
            pe.wait_ge(ot_taken, len(OT_LIST) - 1)
            out_transposes(NT - 1, 3)

            pe.wait_ge(ot_taken, len(OT_LIST))
            pe.wait_ge(exp_done, UNITS)

            def raw_transposes(n, t):
                i = NT * n + t
                pe.wait_ge(x1_done, i + 1)
                if i >= 2:
                    pe.wait_ge(rt_taken, i - 1)
                for c in range(4):
                    k = 4 * n + c
                    mm = pe.transpose(bank(5 + i % 2)[:, P * c:P * (c + 1)], x1[:, t, P * k:P * (k + 1)], ident[:, :])
                mm.then_inc(rt_done, 1)

            def router(n, t):
                i = NT * n + t
                pe.wait_ge(rt_taken, i + 1)
                for c in range(4):
                    k = 4 * n + c
                    mm = pe.matmul(bank(7)[:, NE * t:NE * (t + 1)], x1T[:, i % 2, P * c:P * (c + 1)],
                                   wrm[:, 0 if t < TL else 1, k, :], start=(i == 0 and c == 0), stop=(n == 3 and c == 3),
                                   skip_group_check=True)
                mm.then_inc(logits_done, 1)

            turn = []
            for n in range(4):
                for q in range(4):
                    ring_wait(("out", n, q))
                    w = at(slot_b(("out", n, q)), 4, NB)
                    for j in range(4):
                        e = 4 * q + j
                        for t in range(NT):
                            if e == 0 and n > 0:
                                pe.wait_ge(out_taken, NT * (n - 1) + t + 1)
                            mm = pe.matmul(bank(t), oT[:, e, P * t:P * (t + 1)], w[:, j, :],
                                           start=(e == 0), stop=(e == HEADS - 1))
                            if e == HEADS - 1 and t < NT - 1:
                                mm.then_inc(out_done, 1)
                    if q < 3:
                        mm.then_inc(used, 1)
                    else:
                        mm.then_inc(out_done, 1)
                        pe.wait_ge(out_done, NT * (n + 1))
                        pe.sem_inc(used, 1)
                    if n > 0:
                        if n == 1 and q == 0:
                            pe.wait_ge(router_w, 2)
                        for t in ([q] if q < 3 else [3, 4]):
                            raw_transposes(n - 1, t)
                            turn.append((n - 1, t))
                            if len(turn) > 1:
                                router(*turn.pop(0))
            for t in range(NT):
                raw_transposes(3, t)
                turn.append((3, t))
                router(*turn.pop(0))
            while turn:
                router(*turn.pop(0))
            pe.wait_ge(out_taken, 4 * NT)
            for k in range(KC):
                mm = pe.matmul(bank(0)[0:2, 0:NE], modT[:, 3, :, k], wr[:, k, :], start=(k == 0), stop=(k == KC - 1))
            mm.then_inc(cst_done, 1)
            pe.wait_ge(cst_taken, 1)
            pe.wait_ge(sel_ready, 2)
            for v in range(2):
                mm = pe.matmul(bank(0)[:, NE * v:NE * (v + 1)], sel[:, v, :], cst[:, :], start=True, stop=True,
                               skip_group_check=True)
            mm.then_inc(cst_done, 1)
            pe.wait_ge(aff_ready, 1)
            for t in range(NT):
                mm = pe.transpose(bank(1 + t // 4)[0:NE, P * (t % 4):P * (t % 4 + 1)], aff[:, t, :], ident[:, :])
            mm.then_inc(affT_done, 1)
            pe.wait_ge(topk_ready, 1)
            pe.transpose(bank(3)[0:CAP, 0:NE], vals[:, :], ident[0:NE, 0:NE])
            pe.transpose(bank(3)[0:CAP, NE:2 * NE], idxf[:, :], ident[0:NE, 0:NE]).then_inc(cols_done, 1)
            pe.wait_ge(cols_ready, 1)

            def gathered_transposes():
                for k in range(KC):
                    mm = pe.transpose(bank(4 + k // 6)[:, CAP * (k % 6):CAP * (k % 6 + 1)],
                                      xs[0:CAP, P * k:P * (k + 1)], ident[0:CAP, 0:CAP])
                mm.then_inc(t1_done, 1)

            pe.wait_ge(xs_ready, 1)
            gathered_transposes()
            with pe.Fori(0, NE) as e:
                def slot_wait(j):
                    pe.wait_ge(xlanded[j % RING_E], e * 32 + 16 * (j // RING_E + 1))

                pe.wait_ge(xsT_ready, e + 1)
                for part in range(2):
                    for j in range(8):
                        slot_wait(8 * part + j)
                        w = at(slot_e(8 * part + j), 2, DE)
                        for i in range(2):
                            k = 2 * j + i
                            for h in range(2):
                                mm = pe.matmul(bank(2 * part + h)[0:CAP, :], xsT[:, k, :], w[:, i, NB * h:NB * (h + 1)],
                                               start=(k == 0), stop=(k == KC - 1))
                        mm.then_inc(xused, 1)
                    if part == 0:
                        pe.wait_ge(xs_ready, e + 2)
                        pe.wait_ge(rows_ready, e + 1)
                        gathered_transposes()
                for h in range(2):
                    pe.wait_ge(hid_half, e * 2 + (h + 1))
                    for f in range(4):
                        mm = pe.transpose(bank(h)[:, CAP * f:CAP * (f + 1)], hid[0:CAP, P * (4 * h + f):P * (4 * h + f + 1)],
                                          ident[0:CAP, 0:CAP])
                    mm.then_inc(ht_done, 1)
                pe.wait_ge(t1_scaled, e + 2)
                for f in range(8):
                    if f % 4 == 0:
                        pe.wait_ge(hidT_half, e * 2 + (f // 4 + 1))
                    slot_wait(16 + f)
                    w = at(slot_e(16 + f), 4, NB)
                    for n in range(4):
                        mm = pe.matmul(bank(4 + n)[0:CAP, :], hidT[:, f, :], w[:, n, :], start=(f == 0), stop=(f == 7))
                    mm.then_inc(xused, 1)

        @block.scalar
        def _(act):
            for t in range(NT):
                act.dma_start(xrows[:, t, :], x_dram(t)).then_inc(x_in[t], 16)
            act.wait_ge(xp_taken, 1)
            act.activation(ctmp[:, :], vecT[:, 0:32], ACT.Exp, scale=-1.0).then_inc(silu_exp, 1)
            act.wait_ge(lam_sum, 1)
            act.activation(lame[:, :], lams[:, :], ACT.Exp).then_inc(lam_exp, 1)
            for t in range(NT):
                act.wait_ge(x_in[t], 16)
                if t > 0:
                    act.wait_ge(x_squared, t)
                act.activation(junkA, xrows[:, t, :], ACT.Square, accum_out=ssx[:, t:t + 1]).then_inc(x_squared, 1)

            for m in range(2):
                act.wait_ge(modA_done, m + 1)
                for c in range(4 if m == 0 else 2):
                    ins = act.activation(mrowA[:, m, NB * c:NB * (c + 1)], bank(4 * m + c)[0:2, :], ACT.Copy)
                ins.then_inc(modA_act, 1)

            def block_out(b):
                o = ORDER.index(b)
                former = [x for x in ORDER[:o] if x in ROWS_BLOCKS]
                keys = len([x for x in ORDER[:o] if x in KEY_BLOCKS])
                for t in range(NT):
                    act.wait_ge(proj_done, NT * o + t + 1)
                    vt = t if t < TL else NT
                    if b in (4, 5):
                        act.activation(V[:, vt, (b - 4) * NB:(b - 3) * NB], bank(t), ACT.Copy).then_inc(proj_taken, 1)
                        continue
                    if former:
                        act.wait_ge(xp_done, transposes_before(("rows", former[-1], t)) + 1)
                        if t == TL and keys:
                            act.wait_ge(k_out, 16 * keys)
                    if b == 8:
                        act.activation(V[:, vt, DH * HD:VW], bank(t)[:, KVH * HD:2 * KVH * HD], ACT.Copy)
                        act.activation(prow[:, t, 0:KVH * HD], bank(t)[:, 0:KVH * HD], ACT.Copy)\
                            .then_inc(proj_taken, 1)
                    else:
                        act.activation(prow[:, t, :], bank(t), ACT.Copy).then_inc(proj_taken, 1)

            for step in STEPS:
                if step[0] == "projk" and step[2] == KC - 1:
                    block_out(step[1])
                elif step[0] == "sum":
                    m = step[1]
                    act.wait_ge(sum_done, m - 1)
                    if m > 2:
                        act.wait_ge(mod_stored, 64 * (m - 2))
                    act.activation(mstage, bank(5), ACT.Copy).then_inc(sum_taken, 1)

            def exps(u):
                t, j, comps, keys, _, scale = unit(u)
                act.wait_ge(max_done, u + 1)
                if u >= 2:
                    act.wait_ge(pt_done, u - 1)
                for c in range(comps):
                    ins = act.activation(E[:, u % 2, c, 0:keys], S_ps(u)[:, TOK * c:TOK * c + keys], ACT.Exp,
                                         bias=nmax[:, u % 4, c:c + 1], scale=scale,
                                         accum_out=ssum[:, u % 4, c:c + 1])
                ins.then_inc(exp_done, 1)

            exps(0)
            exps(1)
            for u in range(UNITS):
                if is_diff(u):
                    keys = unit(u)[3]
                    act.wait_ge(pt_done, u + 1)
                    if u >= 2:
                        act.wait_ge(av_done, u - 1)
                    ins = act.activation(PT[:, u % 2, 0:min(keys, LAT)], bank(6)[:, 0:min(keys, LAT)], ACT.Copy)
                    if keys > LAT:
                        ins = act.activation(PT[:, u % 2, LAT:keys], bank(7)[:, 0:keys - LAT], ACT.Copy)
                    ins.then_inc(pt_act, 1)
                if u + 2 < UNITS:
                    exps(u + 2)

            act.wait_ge(av_done, UNITS)
            act.wait_ge(v_out, 32)
            act.wait_ge(mod_stored, 256)
            for t in range(NT):
                act.dma_start(x1[:, t, :], x_dram(t)).then_inc(x_again[t], 16)
            act.wait_ge(ot_taken, len(OT_LIST))
            act.dma_start(G1, mod_d[0].partition_broadcast(P)).then_inc(g1_in, 16)

            sq = 0
            for n in range(4):
                for t in range(NT):
                    i = NT * n + t
                    act.wait_ge(x1_done, i + 1)
                    if i > 0:
                        act.wait_ge(x1_squared, i)
                    act.activation(junkD, x1[:, t, NB * n:NB * (n + 1)], ACT.Square,
                                   accum_out=ss2[:, t, n:n + 1]).then_inc(x1_squared, 1)
            act.wait_ge(rstd2_ready, 1)
            act.wait_ge(out_done, 4 * NT)
            for t in range(NT):
                act.activation(xn[:, t, :], x1[:, t, :], ACT.Copy, scale=rstd2[:, t:t + 1]).then_inc(xn2_ready, 1)
                if t == 0:
                    act.wait_ge(lshift_ready, 1)
                    act.activation(aff[:, :, :], logit[:, :, :], ACT.Exp).then_inc(lexp_done, 1)
                act.wait_ge(xn2_ready, t + 1)
                act.dma_start(xn_d[P * t:P * (t + 1), :], xn[:, t, :]).then_inc(xn_stored[t], 16)
            act.dma_start(G2[0:CL, :], mod_d[3, 0].partition_broadcast(CL)).then_inc(g2_in, 16)
            act.dma_start(G2[CL:CAP, :], mod_d[3, 1].partition_broadcast(CX)).then_inc(g2_in, 16)
            act.wait_ge(cols_ready, 1)
            act.dma_start(fgB, final_g.partition_broadcast(P)).then_inc(fg_in, 16)
            for t in range(NT):
                act.wait_ge(xn_stored[t], 16)
            with act.Fori(0, NE) as e:
                act.wait_ge(xused, e * XCH + 8)
                act.activation(sg[0:CAP, :], bank(0, 2)[0:CAP, :], ACT.Exp, scale=-1.0).then_inc(sig_exp, 1)
                for h in range(2):
                    act.wait_ge(ht_done, e * 2 + (h + 1))
                    act.activation(hidT[:, 4 * h:4 * h + 4, :].rearrange("p f c -> p (f c)"), bank(h)[:, 0:4 * CAP],
                                   ACT.Copy).then_inc(hidT_half, 1)

            for t in range(NT):
                act.wait_ge(acc_in[t], 16)
                if t > 0:
                    act.wait_ge(f_squared, t)
                act.activation(junkF, x1[:, t, :], ACT.Square, accum_out=ssf[:, t:t + 1]).then_inc(f_squared, 1)
            for t in range(NT):
                act.wait_ge(y_ready, t + 1)
                dst = y_sample[0, P * t:P * (t + 1), :] if t < TL else y_prompt[0]
                act.dma_start(dst, x1[:, t, :]).then_inc(y_out, 16)
            act.wait_ge(y_out, 16 * NT)

        @block.gpsimd
        def _(pool):
            def rows16(v):
                return v.rearrange("o (k p) -> (o k) p", p=P)

            pool.dma_start(vrows[0:16, :], rows16(cvec)).then_inc(small_in, 16)
            pool.dma_start(vrows[16:32, :], c_ctx.rearrange("(k p) -> k p", p=P)).then_inc(small_in, 16)
            pool.dma_start(vrows[32:48, :], rows16(norm1_g)).then_inc(small_in, 16)
            pool.dma_start(vrows[48:64, :], rows16(norm2_g)).then_inc(small_in, 16)
            pool.dma_start(vrows[64:65, :], subln_g).then_inc(small_in, 16)
            pool.dma_start(brows[:, :], rows16(b_mod)).then_inc(small_in, 16)
            for i, v in enumerate((lq1, lq2, lk1, lk2)):
                pool.dma_start(lamv[:, i // 2, i % 2, :], v[0].partition_broadcast(P)).then_inc(small_in, 16)
            pool.dma_start(gains[:, 0, :], qn_g[0].partition_broadcast(P)).then_inc(small_in, 16)
            pool.dma_start(gains[:, 1, :], kn_g[0].partition_broadcast(P)).then_inc(small_in, 16)
            pool.memset(ident[:, :], 0.0).then_inc(ident_half, 1)
            pool.wait_ge(ident_half, 1)
            pool.affine_select(out=ident[:, :], in_=ident[:, :], compare_op=ALU.not_equal, fill=1.0, base=0,
                               pattern=[[-1, P]], channel_multiplier=1).then_inc(ident_ready, 1)
            pool.memset(mhalf[:, :], -0.5).then_inc(const_ready, 1)
            pool.memset(selv[:, :, :], 0.0).then_inc(selv_zero, 1)
            pool.wait_ge(selv_zero, 1)
            for v in range(2):
                pool.memset(selv[:, v, v:v + 1], 1.0).then_inc(selv_ready, 1)
            for v in range(2):
                pool.dma_start(mod_d[:, v, :], b_mod[0, 2 * D:].rearrange("(m n) -> m n", m=4)).then_inc(bias_in, 16)
            rope_v = rope.rearrange("(t p) c -> p t c", p=P)
            pool.dma_start(ropeD, rope_v[:, :, 0:2 * DQ].rearrange("p t (s d) -> p t s d", s=2)).then_inc(rope_in, 16)
            pool.dma_start(ropeQ, rope_v[:, :, 2 * DQ:].rearrange("p t (s d) -> p t s d", s=2)).then_inc(rope_in, 16)
            pool.dma_start(cdk_rows, cache_dk.rearrange("b o t h c d -> (b o t) (h c d)")).then_inc(cache_in, 16)
            pool.dma_start(cgk_rows, cache_gk.rearrange("b o t h d -> (b o t) (h d)")).then_inc(cache_in, 16)
            pool.wait_ge(const_ready, 1)

            def power(out, in_, n, done):
                pool.tensor_tensor(out, in_, mhalf[:, 0:n], ALU.pow).then_inc(done, 1)

            pool.wait_ge(ms_ready, 1)
            power(rstd[:, :], ssx[:, :], NT, rstd_ready)
            pool.wait_ge(xp_done, transposes_before(("x", KC - 1)) + 2)
            pool.dma_start(V[:, TL, 0:DH * HD], cache_dv.rearrange("b o t h d -> (b o t) (h d)")).then_inc(v_in, 16)
            pool.dma_start(V[:, TL, DH * HD:VW], cache_gv.rearrange("b o t h d -> (b o t) (h d)")).then_inc(v_in, 16)
            dk_v = new_dk.rearrange("b o t h c d -> (b o t) (h c d)")
            n = stores = 0
            for step in STEPS:
                if step[0] == "sum":
                    m = step[1]
                    if m == 2:
                        pool.wait_ge(bias_in, 32)
                    pool.wait_ge(sum_taken, m - 1)
                    for r in range(4):
                        pool.dma_start(mod_d[m - 2, :, NB * r:NB * (r + 1)], mstage[32 * r:32 * r + 2, :],
                                       accum_op=ALU.add).then_inc(mod_stored, 16)
                if step[0] != "projk" or step[2] < KC - 1:
                    continue
                b = step[1]
                if b >= 6:
                    for t in range(NT):
                        n += 1
                        pool.wait_ge(rowms_ready, n)
                        h = 2 if b == 8 else 4
                        power(rg[:, 0:h], ssg[:, 0:h], h, rowr_ready)
                if b in KEY_BLOCKS:
                    if b == 8:
                        pool.wait_ge(roped, ROPED.index((8, TL)) + 1)
                        dst, src = new_gk.rearrange("b o t h d -> (b o t) (h d)"), prow[:, TL, 0:KVH * HD]
                    else:
                        pool.wait_ge(proj_taken, proj_count(b, TL))
                        dst, src = dk_v[:, (b - 2) * NB:(b - 1) * NB], prow[:, TL, :]
                    stores += 1
                    pool.dma_start(dst, src).then_inc(k_out, 16)
                    pool.wait_ge(k_out, 16 * stores)
            pool.wait_ge(mod_stored, 256)
            for i in range(4):
                pool.dma_start(colrows[16 * i:16 * (i + 1), :],
                               mod_d[1 + i // 2, i % 2].rearrange("(k p) -> k p", p=P)).then_inc(colrows_in, 16)
            pool.wait_ge(proj_taken, proj_count(5, TL))
            pool.dma_start(new_dv.rearrange("b o t h d -> (b o t) (h d)"), V[:, NT, 0:DH * HD]).then_inc(v_out, 16)
            pool.dma_start(new_gv.rearrange("b o t h d -> (b o t) (h d)"), V[:, NT, DH * HD:VW]).then_inc(v_out, 16)
            for t in range(NT):
                pool.wait_ge(oms_ready, t + 1)
                power(ro[:, :], sso[:, :], DH, or_ready)
            pool.wait_ge(ot_taken, len(OT_LIST))
            pool.dma_start(wr, w_router.rearrange("o (k p) e -> p (o k) e", p=P)).then_inc(wr_in, 16)
            pool.wait_ge(x1_done, 4 * NT)
            pool.dma_start(acc_d.rearrange("(t p) n -> p t n", p=P), x1).then_inc(acc_stored, 16)
            pool.wait_ge(ms2_ready, 1)
            power(rstd2[:, :], ms2[:, :], NT, rstd2_ready)

            pool.wait_ge(cols_ready, 1)
            pool.wait_ge(acc_stored, 16)
            for t in range(NT):
                pool.wait_ge(xn_stored[t], 16)

            def gather(e):
                pool.tensor_copy(idxg[:, :], idxC[:, e:e + 1]).then_inc(idx_set, 1)
                pool.wait_ge(idx_set, 1 if e == 0 else 2 * e)
                pool.indirect_dma_start(xs[0:CAP, :], None, xn_d[:, :],
                                        bass.IndirectOffsetOnAxis(ap=idxg[:, 0:1], axis=0)).then_inc(gathered, 16)
                pool.wait_ge(gathered, 16 * (e + 1))
                pool.sem_inc(xs_ready, 1)

            def scatter(e):
                pool.tensor_copy(idxs[:, :], idxC[:, e:e + 1]).then_inc(idx_set, 1)
                pool.wait_ge(idx_set, min(2 * e + 3, 2 * NE))
                pool.wait_ge(rows_ready, e + 2)
                pool.indirect_dma_start(acc_d[:, :], bass.IndirectOffsetOnAxis(ap=idxs[:, 0:1], axis=0),
                                        xrow_out[0:CAP, :], None, compute_op=ALU.add).then_inc(scattered, 16)
                pool.wait_ge(scattered, 16 * (e + 1))
                pool.sem_inc(row_free, 1)

            pool.sem_inc(row_free, 1)
            gather(0)
            for e in range(NE):
                if e + 1 < NE:
                    pool.wait_ge(t1_done, e + 1)
                    gather(e + 1)
                else:
                    pool.sem_inc(xs_ready, 1)
                scatter(e)
            for t in range(NT):
                pool.dma_start(x1[:, t, :], acc_d[P * t:P * (t + 1), :]).then_inc(acc_in[t], 16)
            for t in range(NT):
                pool.wait_ge(fms_ready, t + 1)
                power(rf[:, t:t + 1], ssf[:, t:t + 1], 1, frstd_ready)

        @block.vector
        def _(dve):
            steps = [0]

            def link(ins):
                steps[0] += 1
                ins.then_inc(dve_step, 1)
                dve.wait_ge(dve_step, steps[0])

            def bc(v, n, axis=1):
                shape = list(v.shape)
                shape.insert(axis, n)
                return v.unsqueeze(axis).broadcast_to(shape)

            def take(i):
                dve.wait_ge(xp_done, i + 1)
                return bank(6 + i % 2)

            b = take(0)
            dve.tensor_copy(vecT[:, :], b[:, 0:65]).then_inc(xp_taken, 1)
            b = take(1)
            dve.tensor_copy(bmodT[:, :], b[:, 0:96]).then_inc(xp_taken, 1)
            link(dve.tensor_tensor(lamv[:, 0], lamv[:, 0], lamv[:, 1], ALU.mult))
            dve.tensor_reduce(lams[:, :], lamv[:, 0], AX, ALU.add).then_inc(lam_sum, 1)
            dve.wait_ge(silu_exp, 1)
            link(dve.tensor_scalar(ctmp[:, :], ctmp[:, :], 1.0, None, ALU.add))
            link(dve.reciprocal(ctmp[:, :], ctmp[:, :]))
            dve.tensor_tensor(cT.rearrange("p k v -> p v k"), vecT[:, 0:32].rearrange("p (v k) -> p v k", v=2),
                              ctmp[:, :].rearrange("p (v k) -> p v k", v=2), ALU.mult).then_inc(c_ready, 1)
            dve.wait_ge(lam_exp, 1)
            link(dve.tensor_tensor(neglam[:, :], lame[:, 1:2], lame[:, 0:1], ALU.subtract))
            link(dve.tensor_scalar(neglam[:, :], neglam[:, :], LAM_INIT, None, ALU.subtract))
            dve.wait_ge(rope_in, 32)
            for tab, g in ((ropeK, 1), (ropeQ, 0)):
                gn = gains[:, g, :]
                link(dve.tensor_tensor(tab[:, :, 0, :], ropeQ[:, :, 0, :], bc(gn, TL), ALU.mult))
                gsw = gn.rearrange("p (a h i) -> p a h i", a=2, h=2)
                for h in range(2):
                    for t in range(TL):
                        so = tab[:, t, 1, :].rearrange("p (a h i) -> p a h i", a=2, h=2)
                        si = ropeQ[:, t, 1, :].rearrange("p (a h i) -> p a h i", a=2, h=2)
                        link(dve.tensor_tensor(so[:, :, h, :], si[:, :, h, :], gsw[:, :, 1 - h, :], ALU.mult))
            dve.wait_ge(x_squared, NT)
            dve.tensor_scalar(ssx[:, :], ssx[:, :], 1.0 / D, EPS, ALU.mult, ALU.add).then_inc(ms_ready, 1)
            dve.wait_ge(rstd_ready, 1)
            for t in range(NT):
                dve.tensor_scalar(xrows[:, t, :], xrows[:, t, :], rstd[:, t:t + 1], None, ALU.mult).then_inc(xn_ready, 1)
            dve.wait_ge(modA_done, 2)
            for c in range(2, 4):
                ins = dve.tensor_copy(mrowA[:, 1, NB * c:NB * (c + 1)], bank(4 + c)[0:2, :])
            ins.then_inc(modA_dve, 1)

            n_ms = [0]

            def shape_rows(b, t):
                dve.wait_ge(proj_taken, proj_count(b, t))
                before = [r for r in ROPED if (ORDER.index(r[0]), r[1]) < (ORDER.index(b), t)]
                if before:
                    dve.wait_ge(roped, len(before))
                W = KVH * HD if b == 8 else NB
                v = prow[:, t, 0:W]
                if b >= 6:
                    h = W // HD
                    v3 = v.rearrange("p (h d) -> p h d", h=h)
                    link(dve.tensor_tensor(rz[:, 0:W], v, v, ALU.mult))
                    link(dve.tensor_reduce(ssg[:, 0:h], rz[:, 0:W].rearrange("p (h d) -> p h d", h=h), AX, ALU.add))
                    n_ms[0] += 1
                    dve.tensor_scalar(ssg[:, 0:h], ssg[:, 0:h], 1.0 / HD, EPS, ALU.mult, ALU.add).then_inc(rowms_ready, 1)
                    dve.wait_ge(rowr_ready, n_ms[0])
                    link(dve.tensor_tensor(v3, v3, bc(rg[:, 0:h], HD, 2), ALU.mult))
                    if t == TL:
                        dve.tensor_tensor(v3, v3, bc(gains[:, 1 if b == 8 else 0, :], h), ALU.mult).then_inc(roped, 1)
                        return
                    tab, grp, q = (ropeK if b == 8 else ropeQ)[:, t], h, HD // 4
                else:
                    if t == TL:
                        return
                    tab, grp, q = ropeD[:, t], W // DQ, DQ // 4
                w = 4 * q
                y3, z3, vv = (x_[:, 0:W].rearrange("p (g d) -> p g d", d=w) for x_ in (ry, rz, prow[:, t]))
                dve.tensor_tensor(y3, vv, bc(tab[:, 0, :], grp), ALU.mult)
                for hf in range(2):
                    def half(x_, i):
                        return x_.rearrange("p (g a h i) -> p g a h i", a=2, h=2, i=q)[:, :, :, i, :]
                    s = tab[:, 1, :].rearrange("p (a h i) -> p a h i", a=2, h=2)[:, :, hf, :]
                    ins = dve.tensor_tensor(half(rz[:, 0:W], hf), half(v, 1 - hf), bc(s, grp), ALU.mult)
                link(ins)
                dve.tensor_tensor(v, ry[:, 0:W], rz[:, 0:W], ALU.add).then_inc(roped, 1)

            n_mod = n_rope = 0
            for step in STEPS:
                kind = step[0]
                if kind == "cols":
                    m = step[1]
                    b = take(transposes_before(step))
                    dve.tensor_tensor(modT[:, m], b[:, 0:32].rearrange("p (k v) -> p v k", v=2),
                                      bc(bmodT[:, KC * m:KC * (m + 1)], 2), ALU.add).then_inc(xp_taken, 1)
                    if m == 1:
                        dve.wait_ge(xp_taken, transposes_before(step) + 1)
                        link(dve.scalar_tensor_tensor(out=A1[:, :, :], in0=modT[:, 1], scalar=1.0,
                                                      in1=bc(vecT[:, 32:48], 2), op0=ALU.add, op1=ALU.mult))
                elif kind == "cols2":
                    b = take(transposes_before(step))
                    dve.tensor_copy(modT[:, 3:5], b[:, 0:64].rearrange("p (m v k) -> p m v k", m=2, v=2))\
                        .then_inc(xp_taken, 1)
                    dve.wait_ge(xp_taken, transposes_before(step) + 1)
                    link(dve.scalar_tensor_tensor(out=A2[:, :, :], in0=modT[:, 4], scalar=1.0,
                                                  in1=bc(vecT[:, 48:64], 2), op0=ALU.add, op1=ALU.mult))
                elif kind == "modB":
                    _, m, k = step
                    slot, fill, _ = PLAN[step]
                    dve.wait_ge(landed[slot], 16 * fill)
                    w = at(slot_b(step), D)
                    if k == 0:
                        if m > 2:
                            dve.wait_ge(sum_done, m - 2)
                        else:
                            dve.wait_ge(xp_done, transposes_before(("cols", 1)) + 1)
                    else:
                        dve.wait_ge(mod_used, n_mod)
                    for v in range(2):
                        if k == 0:
                            ins = dve.tensor_scalar(macc[:, v, :], w, cT[:, k, v:v + 1], None, ALU.mult)
                        else:
                            ins = dve.scalar_tensor_tensor(out=macc[:, v, :], in0=w, scalar=cT[:, k, v:v + 1],
                                                           in1=macc[:, v, :], op0=ALU.mult, op1=ALU.add)
                    ins.then_inc(mod_used, 1)
                    n_mod += 1
                elif kind == "cache":
                    h0, n = ((0, 4), (4, 4), (8, 2))[step[1]]
                    b = take(transposes_before(step))
                    dve.tensor_copy(kT[:, h0:h0 + n, LAT:LAT + PAST], b[:, 0:n * HD].rearrange("p (h t) -> p h t", h=n))\
                        .then_inc(xp_taken, 1)
                elif kind == "x":
                    k = step[1]
                    i = transposes_before(step)
                    b = take(i)
                    dve.tensor_scalar(hT[:, k, 0:LAT], b, A1[:, 0, k:k + 1], modT[:, 0, 0, k:k + 1], ALU.mult, ALU.add)\
                        .then_inc(xp_taken, 1)
                    b = take(i + 1)
                    dve.tensor_scalar(hT[:, k, LAT:TOK], b[:, 0:P], A1[:, 1, k:k + 1], modT[:, 0, 1, k:k + 1],
                                      ALU.mult, ALU.add).then_inc(xp_taken, 1)
                elif kind == "projk" and step[2] == KC - 1 and step[1] in ROWS_BLOCKS:
                    for t in range(NT):
                        shape_rows(step[1], t)
                elif kind == "rows":
                    _, blk, t = step
                    b = take(transposes_before(step))
                    if blk in (0, 1):
                        dst = qT[:, 4 * blk:4 * blk + 4, P * t:P * (t + 1)]
                    elif blk in (6, 7):
                        dst = qT[:, DH + 4 * (blk - 6):DH + 4 * (blk - 5), P * t:P * (t + 1)]
                    else:
                        col = P * t if t < TL else LAT + PAST
                        dst = kT[:, 4 * (blk - 2):4 * (blk - 1), col:col + P] if blk < 4 else kT[:, DH:DH + KVH, col:col + P]
                    h = dst.shape[1]
                    dve.tensor_copy(dst, b[:, 0:h * HD].rearrange("p (h t) -> p h t", h=h)).then_inc(xp_taken, 1)

            def maxima(u):
                t, j, comps, keys, _, scale = unit(u)
                dve.wait_ge(scored, u + 1)
                if u >= 1:
                    dve.wait_ge(max_done, u)
                link(dve.tensor_reduce(mx[:, 0:comps],
                                       S_ps(u)[:, 0:2 * TOK].rearrange("p (c k) -> p c k", c=2)[:, 0:comps, 0:keys],
                                       AX, ALU.max))
                dve.tensor_scalar(nmax[:, u % 4, 0:comps], mx[:, 0:comps], -scale, None, ALU.mult).then_inc(max_done, 1)

            def combine(u):
                t, j, comps, keys, _, _ = unit(u)
                dve.wait_ge(exp_done, u + 1)
                if comps == 1:
                    dve.reciprocal(rsum[:, u % 4, 0:1], ssum[:, u % 4, 0:1]).then_inc(probs_ready, 1)
                    return
                if u >= 1:
                    dve.wait_ge(probs_ready, u)
                link(dve.reciprocal(rsum[:, u % 4, :], ssum[:, u % 4, :]))
                link(dve.scalar_tensor_tensor(out=coef[:, :], in0=ssum[:, u % 4, 0:1], scalar=neglam[:, 0:1],
                                              in1=rsum[:, u % 4, 1:2], op0=ALU.mult, op1=ALU.mult))
                dve.scalar_tensor_tensor(out=E[:, u % 2, 0, 0:keys], in0=E[:, u % 2, 1, 0:keys], scalar=coef[:, 0:1],
                                         in1=E[:, u % 2, 0, 0:keys], op0=ALU.mult, op1=ALU.add).then_inc(probs_ready, 1)

            def take_ot(t, r):
                dve.wait_ge(ot_done, OT_LIST.index((t, r)) + 1)
                dst = oT[:, 4 * r:4 * r + 4, P * t:P * (t + 1)]
                src = bank(6).rearrange("p (h t) -> p h t", h=4)
                if r < 2:
                    dve.tensor_scalar(dst, src, vecT[:, 64:65], 1.0 - LAM_INIT, ALU.mult, ALU.mult).then_inc(ot_taken, 1)
                else:
                    dve.tensor_copy(dst, src).then_inc(ot_taken, 1)

            dve.wait_ge(k_out, 48)
            dve.wait_ge(mod_stored, 256)
            dve.wait_ge(colrows_in, 64)
            maxima(0)
            maxima(1)
            combine(0)
            for u in range(UNITS):
                t, j, comps, keys, kh, _ = unit(u)
                if not is_diff(u):
                    dve.wait_ge(pt_done, u + 1)
                    if u >= 2:
                        dve.wait_ge(av_done, u - 1)
                    ins = dve.tensor_copy(PT[:, u % 2, 0:min(keys, LAT)], bank(6)[:, 0:min(keys, LAT)])
                    if keys > LAT:
                        ins = dve.tensor_copy(PT[:, u % 2, LAT:keys], bank(7)[:, 0:keys - LAT])
                    ins.then_inc(pt_dve, 1)
                if u + 1 < UNITS:
                    combine(u + 1)
                if u + 2 < UNITS:
                    maxima(u + 2)
                dve.wait_ge(av_done, u + 1)
                dve.tensor_scalar(orow[:, j, :], bank(7)[:, P:2 * P], rsum[:, u % 4, 0:1], None, ALU.mult)\
                    .then_inc(o_taken, 1)
                if j == DH - 1:
                    dve.wait_ge(o_taken, u + 1)
                    od = orow[:, 0:DH, :]
                    o3 = osq.rearrange("p (h d) -> p h d", h=DH)
                    link(dve.tensor_tensor(o3, od, od, ALU.mult))
                    link(dve.tensor_reduce(sso[:, :], o3, AX, ALU.add))
                    dve.tensor_scalar(sso[:, :], sso[:, :], 1.0 / HD, EPS, ALU.mult, ALU.add).then_inc(oms_ready, 1)
                if j == DH:
                    dve.wait_ge(or_ready, t + 1)
                    dve.tensor_tensor(orow[:, 0:DH, :], orow[:, 0:DH, :], bc(ro[:, :], HD, 2), ALU.mult)\
                        .then_inc(onorm_ready, 1)
                if ot_round(u):
                    take_ot(*ot_round(u))
            take_ot(NT - 1, 2)
            take_ot(NT - 1, 3)

            dve.wait_ge(wr_in, 16)
            for v in range(2):
                dve.tensor_tensor(wrm[:, v], wr[:, :, :], bc(A2[:, v, :], NE, 2), ALU.mult).then_inc(router_w, 1)

            def take_raw(i):
                dve.wait_ge(rt_done, i + 1)
                if i >= 2:
                    dve.wait_ge(logits_done, i - 1)
                dve.tensor_copy(x1T[:, i % 2, :], bank(5 + i % 2)).then_inc(rt_taken, 1)

            dve.wait_ge(g1_in, 16)
            for n in range(4):
                if n > 0:
                    for t in range(NT):
                        take_raw(NT * (n - 1) + t)
                for t in range(NT):
                    i = NT * n + t
                    if n == 0:
                        dve.wait_ge(x_again[t], 16)
                    dve.wait_ge(out_done, i + 1)
                    v = 0 if t < TL else 1
                    cols = slice(NB * n, NB * (n + 1))
                    if i > 0:
                        dve.wait_ge(x1_done, i)
                    dve.tensor_tensor(gtmp, bank(t), G1[:, v, cols], ALU.mult).then_inc(out_taken, 1)
                    dve.wait_ge(out_taken, i + 1)
                    dve.tensor_tensor(x1[:, t, cols], x1[:, t, cols], gtmp, ALU.add).then_inc(x1_done, 1)
            for t in range(NT):
                take_raw(3 * NT + t)
            for v in range(2):
                dve.tensor_copy(sel[:, v, :], ident[0:2, v:v + 1].broadcast_to([2, P])).then_inc(sel_ready, 1)
            dve.wait_ge(cst_done, 1)
            dve.tensor_copy(cst[:, :], bank(0)[0:2, 0:NE]).then_inc(cst_taken, 1)
            dve.wait_ge(x1_squared, 4 * NT)
            link(dve.tensor_reduce(ms2[:, :], ss2[:, :, :], AX, ALU.add))
            dve.tensor_scalar(ms2[:, :], ms2[:, :], 1.0 / D, EPS, ALU.mult, ALU.add).then_inc(ms2_ready, 1)
            dve.wait_ge(cst_done, 2)
            link(dve.tensor_copy(cstB[:, :, :], bank(0)[:, 0:2 * NE].rearrange("p (v e) -> p v e", v=2)))
            dve.wait_ge(rstd2_ready, 1)
            dve.wait_ge(logits_done, 4 * NT)
            for t in range(NT):
                ins = dve.scalar_tensor_tensor(out=logit[:, t, :], in0=bank(7)[:, NE * t:NE * (t + 1)],
                                               scalar=rstd2[:, t:t + 1], in1=cstB[:, 0 if t < TL else 1, :],
                                               op0=ALU.mult, op1=ALU.add)
            link(ins)
            link(dve.tensor_reduce(lmax[:, :], logit[:, :, :], AX, ALU.max))
            dve.tensor_tensor(logit[:, :, :], logit[:, :, :], bc(lmax[:, :], NE, 2), ALU.subtract).then_inc(lshift_ready, 1)
            dve.wait_ge(lexp_done, 1)
            link(dve.tensor_reduce(lmax[:, :], aff[:, :, :], AX, ALU.add))
            link(dve.reciprocal(lmax[:, :], lmax[:, :]))
            dve.tensor_tensor(aff[:, :, :], aff[:, :, :], bc(lmax[:, :], NE, 2), ALU.mult).then_inc(aff_ready, 1)
            dve.wait_ge(affT_done, 1)
            link(dve.tensor_copy(affT[:, 0:LAT], bank(1)[0:NE, :]))
            link(dve.tensor_copy(affT[:, LAT:TOK], bank(2)[0:NE, 0:CTX]))
            for lo, hi, at0, count in ((0, LAT, 0, CL), (LAT, TOK, CL, CX)):
                row = affT[:, lo:hi]
                for r in range(count // 8):
                    top = slice(at0 + 8 * r, at0 + 8 * r + 8)
                    link(dve.max(vals[:, top], row))
                    link(dve.max_index(idx[:, top], vals[:, top], row))
                    if r < count // 8 - 1:
                        link(dve.match_replace(row, vals[:, top], row, -1.0))
            link(dve.tensor_copy(idxf[:, :], idx[:, :]))
            dve.tensor_scalar(idxf[:, CL:CAP], idxf[:, CL:CAP], float(LAT), None, ALU.add).then_inc(topk_ready, 1)
            dve.wait_ge(cols_done, 1)
            link(dve.tensor_copy(gateC[:, :], bank(3)[0:CAP, 0:NE]))
            dve.tensor_copy(idxC[:, :], bank(3)[0:CAP, NE:2 * NE]).then_inc(cols_ready, 1)
            for t in range(NT):
                dve.wait_ge(xn_stored[t], 16)

            lat, con = slice(0, CL), slice(CL, CAP)
            kinds = ((0, lat), (1, con))
            groups = [(g, min(6, KC - 6 * g)) for g in range(3)]

            def scale_rows():
                for g, n in groups:
                    src = bank(4 + g)[:, 0:n * CAP].rearrange("p (k c) -> p k c", k=n)
                    for v, cs in kinds:
                        ins = dve.tensor_tensor(xstage[:, 6 * g:6 * g + n, cs], src[:, :, cs],
                                                bc(A2[:, v, 6 * g:6 * g + n], cs.stop - cs.start, 2), ALU.mult)
                ins.then_inc(t1_scaled, 1)

            def shift_rows():
                for v, cs in kinds:
                    ins = dve.tensor_tensor(xsT[:, :, cs], xstage[:, :, cs], bc(modT[:, 3, v, :], cs.stop - cs.start, 2),
                                            ALU.add)
                ins.then_inc(xsT_ready, 1)

            dve.sem_inc(rows_ready, 1)
            dve.wait_ge(t1_done, 1)
            scale_rows()
            dve.wait_ge(t1_scaled, 1)
            shift_rows()
            dve.wait_ge(g2_in, 32)
            with dve.Fori(0, NE) as e:
                dve.wait_ge(sig_exp, e + 1)
                dve.tensor_scalar(sg[0:CAP, :], sg[0:CAP, :], 1.0, None, ALU.add).then_inc(sig_add, 1)
                dve.wait_ge(sig_add, e + 1)
                dve.reciprocal(sg[0:CAP, :], sg[0:CAP, :]).then_inc(sig_rec, 1)
                dve.wait_ge(sig_rec, e + 1)
                dve.tensor_tensor(sg[0:CAP, :], bank(0, 2)[0:CAP, :], sg[0:CAP, :], ALU.mult).then_inc(sig_mul, 1)
                dve.wait_ge(t1_done, e + 2)
                dve.wait_ge(xsT_ready, e + 1)
                scale_rows()
                dve.wait_ge(sig_mul, e + 1)
                dve.wait_ge(xused, e * XCH + 16)
                for h in range(2):
                    cs = slice(NB * h, NB * (h + 1))
                    dve.tensor_tensor(hid[0:CAP, cs], bank(2 + h)[0:CAP, :], sg[0:CAP, cs], ALU.mult).then_inc(hid_half, 1)
                dve.wait_ge(t1_scaled, e + 2)
                shift_rows()
                dve.wait_ge(rows_ready, e + 1)
                dve.tensor_copy(gcol[:, :], gateC[:, bass.ds(e, 1)]).then_inc(gcol_ready, 1)
                dve.wait_ge(gcol_ready, e + 1)
                dve.wait_ge(row_free, e + 1)
                dve.wait_ge(xused, e * XCH + 24)
                for n in range(4):
                    cs = slice(NB * n, NB * (n + 1))
                    ins = dve.scalar_tensor_tensor(out=xrow_out[0:CAP, cs], in0=bank(4 + n)[0:CAP, :], scalar=gcol[:, 0:1],
                                                   in1=G2[0:CAP, cs], op0=ALU.mult, op1=ALU.mult)
                ins.then_inc(rows_ready, 1)

            dve.wait_ge(fg_in, 16)
            for t in range(NT):
                dve.wait_ge(f_squared, t + 1)
                dve.tensor_scalar(ssf[:, t:t + 1], ssf[:, t:t + 1], 1.0 / D, EPS, ALU.mult, ALU.add).then_inc(fms_ready, 1)
                dve.wait_ge(frstd_ready, t + 1)
                dve.scalar_tensor_tensor(out=x1[:, t, :], in0=x1[:, t, :], scalar=rf[:, t:t + 1], in1=fgB,
                                         op0=ALU.mult, op1=ALU.mult).then_inc(y_ready, 1)


def rope_tables():
    t = np.arange(LAT)
    row, col = (t // GRID_W).astype(np.float32), (t % GRID_W).astype(np.float32)
    cols = []
    for dim in (DQ, HD):
        sec = dim // 2
        inv = (10000.0 ** (-np.arange(0, sec, 2, dtype=np.float32) / sec)).astype(np.float32)
        ang = np.stack([row[:, None] * inv, col[:, None] * inv], axis=1)
        sign = np.array([-1.0, 1.0], np.float32)[None, None, :, None]
        both = np.stack([ang, ang], axis=2)
        cols += [np.cos(both).reshape(LAT, dim), (np.sin(both) * sign).reshape(LAT, dim)]
    return np.concatenate(cols, axis=1).astype(np.float32)


_INS = ["x_prompt", "x_sample", "c", "cache_diff_k", "cache_diff_v", "cache_gqa_k", "cache_gqa_v", "c_ctx",
        "norm1_g", "norm2_g", "w_mod", "b_mod", "w_in", "w_out", "diff_lambda_q1", "diff_lambda_k1",
        "diff_lambda_q2", "diff_lambda_k2", "diff_subln_g", "gqa_q_norm_g", "gqa_k_norm_g", "w_router",
        "w_expert_gate", "w_expert_up", "w_expert_down", "final_norm_g"]
_OUTS = [(1, CTX, D), (1, LAT, D), (1, 1, CTX, DH, 2, DQ), (1, 1, CTX, DH, HD), (1, 1, CTX, KVH, HD),
         (1, 1, CTX, KVH, HD)]


def kernel(**inputs):
    import concourse.bacc as _bacc
    from concourse.bass_utils import run_bass_kernel_spmd as _run

    nc = _bacc.Bacc("TRN2", target_bir_lowering=False, num_devices=1)
    arrays, args = {}, []
    for name in _INS:
        v = np.ascontiguousarray(inputs[name])
        arrays[f"in_{name}"] = v
        args.append(nc.dram_tensor(f"in_{name}", v.shape, F32, kind="ExternalInput").ap())
    arrays["in_rope"] = rope_tables()
    rope = nc.dram_tensor("in_rope", arrays["in_rope"].shape, F32, kind="ExternalInput").ap()
    outs = [nc.dram_tensor(f"out_{i}", s, F32, kind="ExternalOutput").ap() for i, s in enumerate(_OUTS)]
    build(nc, args, rope, outs)
    r = _run(nc, [arrays], core_ids=[0])
    return tuple(r.results[0][f"out_{i}"] for i in range(len(_OUTS)))
```

```python
import math
from contextlib import ExitStack

import numpy as np

import concourse.bass as bass
from concourse import mybir
from concourse.alu_op_type import AluOpType as ALU

F32 = mybir.dt.float32
F32R = mybir.dt.float32r
BF16 = mybir.dt.bfloat16
U32 = mybir.dt.uint32
ACT = mybir.ActivationFunctionType
AX = mybir.AxisListType.X

P = 128
D = 2048
KC = D // P
LAT, CTX = 512, 128
TOK = LAT + CTX
NT = TOK // P
TL = LAT // P
PAST = 128
NB = 512
HD = 128
DH, GH, KVH = 8, 8, 2
HEADS = DH + GH
GRP = GH // KVH
PROJ = 4608
VW = DH * HD + KVH * HD
NE = 16
DE = 1024
CL, CX = 2 * LAT // NE, 2 * CTX // NE
CAP = CL + CX
EPS = 1e-6
LAM_INIT = 0.8 - 0.6 * math.exp(-0.3 * 0)
GRID_W = 64
DQ = HD // 2
SLOT = 2048
RING_B = 4
X_B, W_B = 3, 4
RING_E = 8
HI_E = 4
HI_D = 3
SPLIT = 1536
XCH = 24
ORDER = [8, 6, 7, 2, 3, 4, 0, 1, 5]
ROWS_BLOCKS = [b for b in ORDER if b not in (4, 5)]
KEY_BLOCKS = (8, 2, 3)
MOD_PACE = [(2, 3, 3, 3), (0, 2, 3, 3), (0, 1, 3, 3), (0, 1, 3, 3), (0, 2, 3, 3), (1, 2, 2, 3), (2, 2, 3, 3), (0, 1, 2, 2)]
assert sum(map(sum, MOD_PACE)) == 4 * KC
UNITS = NT * HEADS


def tensor_steps():
    steps = [("vectors",), ("bmod",)]
    steps += [("modA", m, k) for m in range(2) for k in range(KC)]
    steps += [("cols", 0), ("cols", 1)] + [("x", k) for k in range(3)]
    late = [("modB", m, k) for m in range(2, 6) for k in range(KC)]
    sums = []
    for p, b in enumerate(ORDER):
        for q in range(4):
            pace = MOD_PACE[p][q] if p < len(MOD_PACE) else 0
            for j in range(4):
                k = 4 * q + j
                if p == 0 and k + 3 < KC:
                    steps.append(("x", k + 3))
                steps.append(("projk", b, k))
                sums = [(n - 1, m) for n, m in sums]
                steps += [("sum", m) for n, m in sums if n == 0]
                sums = [x for x in sums if x[0] > 0]
                if j >= 4 - pace:
                    steps.append(late.pop(0))
                    if steps[-1][2] == KC - 1:
                        sums.append((2, steps[-1][1]))
                if p > 0 and ORDER[p - 1] in ROWS_BLOCKS and k >= 6 and k % 2 == 0:
                    steps.append(("rows", ORDER[p - 1], (k - 6) // 2))
                if p == 1 and k == 3:
                    steps += [("cache", i) for i in range(3)]
                if p == len(ORDER) - 1 and k == 5:
                    steps.append(("cols2",))
    return steps


STEPS = tensor_steps()


def plan_loads():
    proj = [("proj", b, q) for b in ORDER for q in range(4)]
    beside, j = {}, -1
    for s in STEPS:
        if s[0] == "projk" and s[2] % 4 == 0:
            j += 1
        if s[0] == "modB":
            beside.setdefault(j, []).append(s)
    order = [s for s in STEPS if s[0] == "modA"] + [proj[0]]
    for j in range(len(proj)):
        order += proj[j + 1:j + 2] + beside.get(j, [])
    order += [("out", n, q) for n in range(4) for q in range(4)]
    counts = {"modA": 0, "proj": 0, "modB": 0, "out": 0}
    former = {"modA": lambda n: ("used", n), "proj": lambda n: ("k_used", 4 * n), "modB": lambda n: ("mod_used", n),
              "out": lambda n: ("used", 2 * KC + n)}
    fills, last, plan = [0] * RING_B, [None] * RING_B, {}
    for c in order:
        kind, n = c[0], counts[c[0]]
        counts[kind] += 1
        slot = {"modA": n % 4, "proj": n % 2, "modB": 2 + n % 2, "out": n % 4}[kind]
        before = last[slot]
        fills[slot] += 1
        last[slot] = former[kind](n + 1)
        plan[c] = (slot, fills[slot], before)
    return order, plan, last


LOADS, PLAN, LAST_USE = plan_loads()
XP = [s for s in STEPS if s[0] in ("vectors", "bmod", "cache", "x", "rows", "cols", "cols2")]


def transposes_before(step):
    n = 0
    for s in XP:
        if s == step:
            return n
        n += 2 if s[0] == "x" else 1


XP_TOTAL = sum(2 if s[0] == "x" else 1 for s in XP)
ROPED = [(b, t) for b in ROWS_BLOCKS for t in range(NT) if b >= 6 or t < TL]


def proj_count(b, t):
    return ORDER.index(b) * NT + t + 1


def build(nc, a, rope, outs):
    (x_prompt, x_sample, cvec, cache_dk, cache_dv, cache_gk, cache_gv, c_ctx, norm1_g, norm2_g, w_mod, b_mod,
     w_in, w_out, lq1, lk1, lq2, lk2, subln_g, qn_g, kn_g, w_router, w_gate, w_up, w_down, final_g) = a
    y_prompt, y_sample, new_dk, new_dv, new_gk, new_gv = outs

    ctx = ExitStack()
    with ctx:
        def sb(name, shape, dt=F32):
            return ctx.enter_context(nc.sbuf_tensor(name, shape, dt))

        def sem(name):
            return ctx.enter_context(nc.semaphore(name))

        acc_d = nc.dram_tensor("acc_d", [TOK, D], F32, kind="Internal").ap()
        xn_d = nc.dram_tensor("xn_d", [TOK, D], F32, kind="Internal").ap()
        gv_d = nc.dram_tensor("gv_d", [TOK, KVH * HD], F32, kind="Internal").ap()
        dv_d = nc.dram_tensor("dv_d", [TOK, NB], F32, kind="Internal").ap()
        mod_d = nc.dram_tensor("mod_d", [4, 2, D], F32, kind="Internal").ap()

        H0 = 0
        R0 = H0 + KC * TOK
        Q0 = R0 + RING_B * SLOT
        K0 = Q0 + HEADS * TOK
        V0 = K0 + (DH + KVH) * (TOK + PAST)
        S0 = V0 + (NT + 1) * VW
        X0 = R0 + (RING_E + HI_E) * SLOT
        W0 = X0 + NT * D
        T0 = S0 + 7040
        END = T0 + 2 * NB
        assert S0 >= X0 and T0 - W0 >= 5632

        def rounded_views(stage, runs):
            views = {}
            with ExitStack() as laid:
                for name, count, words in runs:
                    views[name] = [laid.enter_context(nc.sbuf_tensor(f"{stage}_{name}{i}", [P, words], F32R))
                                   for i in range(count)]
            return views

        XB = V0 + 2560
        parts_B = rounded_views("B", [("hT", 1, R0), ("w_lo", 2, SLOT), ("between", 1, XB - R0 - 2 * SLOT),
                                      ("x_hi", X_B, TOK), ("x_lo", X_B, TOK), ("w_hi", W_B // 2, NB),
                                      ("scratch", 1, T0 - XB - 2 * X_B * TOK - W_B // 2 * NB),
                                      ("w_hi_too", W_B // 2, NB)])
        assert XB + 2 * X_B * TOK + W_B // 2 * NB <= S0
        parts_D = rounded_views("D", [("oT_lo", HEADS, TOK), ("w_lo", RING_B, SLOT), ("oT_hi", HEADS, TOK),
                                      ("w_hi", HI_D, SLOT)])
        parts_E = rounded_views("E", [("xs_and_stage", 1, 3328), ("xsT_hi", 1, KC * CAP), ("xsT_lo", 1, KC * CAP),
                                      ("sg", 1, DE), ("hidT_hi", 1, DE // P * CAP), ("hidT_lo", 1, DE // P * CAP),
                                      ("xrow_out", 1, D), ("w_lo", RING_E, SLOT), ("w_hi", HI_E, SLOT)])
        arena = sb("arena", [P, END])

        def at(off, *dims):
            v = arena[:, off:off + int(np.prod(dims))]
            if len(dims) == 2:
                v = v.rearrange("p (a b) -> p a b", a=dims[0])
            elif len(dims) == 3:
                v = v.rearrange("p (a b c) -> p a b c", a=dims[0], b=dims[1])
            elif len(dims) == 4:
                v = v.rearrange("p (a b c d) -> p a b c d", a=dims[0], b=dims[1], c=dims[2])
            return v

        hT = at(H0, KC, TOK)
        oT = at(H0, HEADS, TOK)
        xrows = at(K0, NT, D)
        mrowA = at(Q0, 2, D)[0:2]
        maccs = {m: (at(Q0, D), at(Q0 + D, D)) if m == 2 else (at(Q0 + 2560, D), at(V0, D)) for m in range(2, 6)}
        cdk_rows = at(Q0 + 4096, DH * HD)
        cgk_rows = at(Q0 + 4096 + DH * HD, KVH * HD)
        vrows = at(Q0 + 5376, P)[0:65, :]
        brows = at(Q0 + 5504, P)[0:96, :]
        lamv = at(Q0 + 5632, 2, 2, DQ)
        junkA = at(Q0 + 8192, D)
        qT = at(Q0, HEADS, TOK)
        kT = at(K0, DH + KVH, TOK + PAST)
        V = at(V0, NT + 1, VW)
        ropeD = at(S0, TL, 2, DQ)
        ropeQ = at(S0 + 512, TL, 2, HD)
        ropeK = at(S0 + 1536, TL, 2, HD)
        prow = at(S0 + 2560, NT, NB)
        ry = at(S0 + 5120, NB)
        rz = at(S0 + 5632, NB)
        E = at(S0, 2, 2, TOK)
        PT = at(S0 + 2560, 2, TOK)
        orow = at(S0 + 3840, HEADS, HD)
        osq = at(S0 + 5888, DH * HD)
        x1 = at(X0, NT, D)
        G1 = at(W0, 2, D)
        gtmp = at(W0 + 4096, NB)
        junkD = at(W0 + 4608, NB // 2).bitcast(BF16)
        wr = at(W0 + 4864, KC, NE)
        wrm = at(W0 + 5120, 2, KC, NE)
        x1T = at(T0, 2, 4 * P)
        xn = at(H0, NT, D)
        oT_hi, oT_lo = parts_D["oT_hi"], parts_D["oT_lo"]
        assert Q0 + HEADS * TOK + HI_D * SLOT <= X0
        xs = at(H0, D)
        xstage = at(H0 + 2048, KC, CAP)
        xsT_hi, xsT_lo = (parts_E[x][0][:, :].rearrange("p (k c) -> p k c", k=KC) for x in ("xsT_hi", "xsT_lo"))
        sg = at(H0 + 5888, DE)
        hidT_hi, hidT_lo = (parts_E[x][0][:, :].rearrange("p (f c) -> p f c", f=DE // P)
                            for x in ("hidT_hi", "hidT_lo"))
        xrow_out = at(H0 + 8192, D)
        G2 = at(W0 + 2048, D)
        fgB = at(W0, D)
        junkF = at(R0, D)

        ident = sb("ident", [P, P])
        vecT = sb("vecT", [P, 65])
        bmodT = sb("bmodT", [P, 96])
        cT = sb("cT", [P, KC, 2])
        ctmp = sb("ctmp", [P, 32])
        modT = sb("modT", [P, 6, 2, KC])
        A1 = sb("A1", [P, 2, KC])
        A2 = sb("A2", [P, 2, KC])
        colrows = at(S0 + 6400, P)[0:64, :]
        mstage = at(S0 + 6528, NB)
        selv = sb("selv", [P, 2, 32])
        gains = at(S0 + 6144, 2, HD)
        lams = sb("lams", [P, 2])
        lame = sb("lame", [P, 2])
        neglam = sb("neglam", [P, 1])
        mhalf = sb("mhalf", [P, 8])
        ssx = sb("ssx", [P, NT])
        rstd = sb("rstd", [P, NT])
        ssg = sb("ssg", [P, NT, 4])
        rg = sb("rg", [P, NT, 4])
        mx = sb("mx", [P, 2])
        nmax = sb("nmax", [P, 4, 2])
        ssum = sb("ssum", [P, 4, 2])
        rsum = sb("rsum", [P, 4, 2])
        coef = sb("coef", [P, 1])
        sso = sb("sso", [P, DH])
        ro = sb("ro", [P, DH])
        ss2 = sb("ss2", [P, NT, 4])
        ms2 = sb("ms2", [P, NT])
        rstd2 = sb("rstd2", [P, NT])
        sel = at(W0 + 1024, 2, P)[0:2]
        cst = sb("cst", [2, NE])
        cstB = sb("cstB", [P, 2, NE])
        logit = at(W0 + 5632, NT, NE)
        aff = at(W0 + 5632 + NT * NE, NT, NE)
        lmax = sb("lmax", [P, NT])
        affT = at(W0, TOK)[0:NE, :]
        vals = at(W0 + TOK, CAP)[0:NE, :]
        idx = at(W0 + TOK + CAP, CAP)[0:NE, :].bitcast(U32)
        idxf = at(W0 + TOK + 2 * CAP, CAP)[0:NE, :]
        gateC = sb("gateC", [CAP, NE])
        idxC = sb("idxC", [CAP, NE + 1], U32)
        gcol = sb("gcol", [CAP, 1])
        idxg = sb("idxg", [CAP, 1], U32)
        idxs = sb("idxs", [CAP, 1], U32)
        ssf = sb("ssf", [P, NT])
        rf = sb("rf", [P, NT])
        flag = sb("flag", [P, 1])

        ps = ctx.enter_context(nc.psum_tensor("ps", [P, 8 * 512], F32))

        def bank(i, n=1):
            return ps[:, 512 * i:512 * (i + n)]

        landed = [sem(f"landed{i}") for i in range(RING_B)]
        used = sem("used")
        mod_used = sem("mod_used")
        xlanded = [sem(f"xlanded{i}") for i in range(RING_E)]
        xused = sem("xused")
        o_hi = sem("o_hi")
        o_lo = sem("o_lo")
        wo_hi = sem("wo_hi")
        wo_lo = sem("wo_lo")
        xw_hi = sem("xw_hi")
        xw_lo = sem("xw_lo")
        xw_lo2 = sem("xw_lo2")
        turn_taken = sem("turn_taken")
        xsum_ready = sem("xsum_ready")
        xhi_ready = sem("xhi_ready")
        hidT_low = sem("hidT_low")
        x_in = [sem(f"x_in{t}") for t in range(NT)]
        small_in = sem("small_in")
        rope_in = sem("rope_in")
        cache_in = sem("cache_in")
        v_in = sem("v_in")
        ident_half = sem("ident_half")
        ident_ready = sem("ident_ready")
        const_ready = sem("const_ready")
        dve_step = sem("dve_step")
        x_squared = sem("x_squared")
        ms_ready = sem("ms_ready")
        rstd_ready = sem("rstd_ready")
        xn_ready = sem("xn_ready")
        silu_exp = sem("silu_exp")
        lam_sum = sem("lam_sum")
        lam_exp = sem("lam_exp")
        c_ready = sem("c_ready")
        xp_done = sem("xp_done")
        xp_taken = sem("xp_taken")
        modA_done = sem("modA_done")
        modA_act = sem("modA_act")
        modA_dve = sem("modA_dve")
        A1_ready = sem("A1_ready")
        selv_zero = sem("selv_zero")
        selv_ready = sem("selv_ready")
        bias_in = sem("bias_in")
        sum_done = sem("sum_done")
        sum_taken = sem("sum_taken")
        mod_stored = sem("mod_stored")
        colrows_in = sem("colrows_in")
        pb_hi = sem("pb_hi")
        pb_lo = sem("pb_lo")
        k_used = sem("k_used")
        val_out = sem("val_out")
        proj_done = sem("proj_done")
        proj_taken = sem("proj_taken")
        rowms_ready = sem("rowms_ready")
        rowr_ready = sem("rowr_ready")
        roped = sem("roped")
        k_out = sem("k_out")
        v_out = sem("v_out")
        gk_normed = sem("gk_normed")
        g1_in = sem("g1_in")
        scored = sem("scored")
        tail_scored = sem("tail_scored")
        max_done = sem("max_done")
        exp_done = sem("exp_done")
        probs_ready = sem("probs_ready")
        pt_done = sem("pt_done")
        pt_act = sem("pt_act")
        pt_dve = sem("pt_dve")
        av_done = sem("av_done")
        o_taken = sem("o_taken")
        oms_ready = sem("oms_ready")
        or_ready = sem("or_ready")
        onorm_ready = sem("onorm_ready")
        ot_done = sem("ot_done")
        ot_taken = sem("ot_taken")
        x_again = [sem(f"x_again{t}") for t in range(NT)]
        out_done = sem("out_done")
        out_taken = sem("out_taken")
        x1_done = sem("x1_done")
        x1_squared = sem("x1_squared")
        rt_done = sem("rt_done")
        rt_taken = sem("rt_taken")
        logits_done = sem("logits_done")
        router_w = sem("router_w")
        wr_in = sem("wr_in")
        sel_ready = sem("sel_ready")
        cst_done = sem("cst_done")
        cst_taken = sem("cst_taken")
        ms2_ready = sem("ms2_ready")
        rstd2_ready = sem("rstd2_ready")
        lshift_ready = sem("lshift_ready")
        lexp_done = sem("lexp_done")
        aff_ready = sem("aff_ready")
        affT_done = sem("affT_done")
        topk_ready = sem("topk_ready")
        cols_done = sem("cols_done")
        cols_ready = sem("cols_ready")
        xn2_ready = sem("xn2_ready")
        xn_stored = [sem(f"xn_stored{t}") for t in range(NT)]
        acc_stored = sem("acc_stored")
        fg_in = sem("fg_in")
        g2_in = sem("g2_in")
        idx_set = sem("idx_set")
        gathered = sem("gathered")
        t1_done = sem("t1_done")
        t1_scaled = sem("t1_scaled")
        xsT_ready = sem("xsT_ready")
        sig_exp = sem("sig_exp")
        sig_add = sem("sig_add")
        sig_rec = sem("sig_rec")
        sig_mul = sem("sig_mul")
        hid_half = sem("hid_half")
        ht_done = sem("ht_done")
        hidT_half = sem("hidT_half")
        gcol_ready = sem("gcol_ready")
        rows_ready = sem("rows_ready")
        scattered = sem("scattered")
        row_free = sem("row_free")
        xs_ready = sem("xs_ready")
        acc_in = [sem(f"acc_in{t}") for t in range(NT)]
        f_squared = sem("f_squared")
        fms_ready = sem("fms_ready")
        frstd_ready = sem("frstd_ready")
        y_ready = sem("y_ready")
        y_out = sem("y_out")

        N_SMALL = 12

        w_mod_v = w_mod.rearrange("o (k p) n -> (o k) p n", p=P)
        w_in_v = w_in.rearrange("o (q j p) n -> (o q) p j n", j=4, p=P)
        w_out_v = w_out.rearrange("o (q j p) n -> (o q) p j n", j=4, p=P)
        wg_v = w_gate.rearrange("o e (j i p) n -> (o e) j p i n", i=2, p=P)
        wu_v = w_up.rearrange("o e (j i p) n -> (o e) j p i n", i=2, p=P)
        wd_v = w_down.rearrange("o e (f p) n -> (o e) f p n", p=P)

        def slot_b(c):
            return R0 + PLAN[c][0] * SLOT

        def slot_e(j):
            return R0 + (j % RING_E) * SLOT

        def split_e(j):
            return parts_E["w_hi"][j % HI_E], parts_E["w_lo"][j % RING_E]

        def out_chunk(i):
            c = ("out", i // 4, i % 4)
            return at(slot_b(c), D), parts_D["w_hi"][i % HI_D], parts_D["w_lo"][PLAN[c][0]], c

        OUT_USED = 2 * KC
        assert LAST_USE == [("used", OUT_USED + 13 + i) for i in range(4)]

        PK = [(b, k) for b in ORDER for k in range(KC)]

        def split_b(s):
            b, k = PK[s]
            c = ("proj", b, k // 4)
            w_hi = (parts_B["w_hi"] + parts_B["w_hi_too"])[s % W_B]
            w_lo = parts_B["w_lo"][PLAN[c][0]]
            return ((hT[:, k, :], at(slot_b(c), 4, NB)[:, k % 4, :]), (parts_B["x_hi"][s % X_B][:, :], w_hi[:, :]),
                    (parts_B["x_lo"][s % X_B][:, :], w_lo[:, NB * (k % 4):NB * (k % 4 + 1)]))

        def three_products(eng, out, x_parts, w_parts, start, stop):
            (x_hi, x_lo), (w_hi, w_lo) = x_parts, w_parts
            eng.matmul(out, x_hi, w_hi, start=start, stop=False)
            eng.matmul(out, x_lo, w_hi, start=False, stop=False)
            return eng.matmul(out, x_hi, w_lo, start=False, stop=stop)

        def x_dram(t):
            return x_sample[0, P * t:P * (t + 1), :] if t < TL else x_prompt[0]

        def unit(u):
            t, j = u // HEADS, u % HEADS
            nc_, keys = (2 if j < DH else 1), (LAT + PAST if t < TL else CTX)
            kh = j if j < DH else DH + (j - DH) // GRP
            scale = (DQ if j < DH else HD) ** -0.5
            return t, j, nc_, keys, kh, scale

        def is_diff(u):
            return u % HEADS < DH

        def diff_before(u):
            return (u // HEADS) * DH + min(u % HEADS, DH)

        def pt_copied(eng, u):
            if is_diff(u):
                eng.wait_ge(pt_act, diff_before(u + 1))
            else:
                eng.wait_ge(pt_dve, u + 1 - diff_before(u + 1))

        def ot_round(u):
            t, j = u // HEADS, u % HEADS
            if j in (11, 13):
                return t, (j - 11) // 2
            if j in (1, 3) and t > 0:
                return t - 1, 2 + (j - 1) // 2
            return None

        OT_LIST = [ot_round(u) for u in range(UNITS) if ot_round(u)] + [(NT - 1, 2), (NT - 1, 3)]

        def S_ps(u):
            return bank(3 * (u % 2), 3)

        block = ctx.enter_context(nc.Block())

        @block.sync
        def _(sp):
            def chunk_b(c):
                slot, _, before = PLAN[c]
                if before:
                    sp.wait_ge({"used": used, "k_used": k_used, "mod_used": mod_used}[before[0]], before[1])
                if c[0] in ("modA", "modB"):
                    sp.dma_start(at(slot_b(c), D), w_mod_v[c[2], :, c[1] * D:(c[1] + 1) * D]).then_inc(landed[slot], 16)
                else:
                    src = w_in_v if c[0] == "proj" else w_out_v
                    sp.dma_start(at(slot_b(c), 4, NB), src[c[2], :, :, c[1] * NB:(c[1] + 1) * NB])\
                        .then_inc(landed[slot], 16)

            def chunk_e(e, j):
                s = slot_e(j)
                if j < 16:
                    w = wg_v if j < 8 else wu_v
                    src = w[bass.ds(e, 1), j % 8].rearrange("e p i n -> (e p) i n")
                    sp.dma_start(at(s, 2, DE), src).then_inc(xlanded[j % RING_E], 16)
                else:
                    src = wd_v[bass.ds(e, 1), j - 16].rearrange("e p n -> (e p) n")
                    sp.dma_start(at(s, D), src).then_inc(xlanded[j % RING_E], 16)

            for c in LOADS:
                chunk_b(c)
            for j in range(RING_E):
                sp.wait_ge(used, LAST_USE[min(j, RING_B - 1)][1])
                chunk_e(0, j)
            for j in range(RING_E, XCH):
                sp.wait_ge(xused, HI_E + j - RING_E + 1)
                chunk_e(0, j)
            with sp.Fori(1, NE) as e:
                for j in range(XCH):
                    sp.wait_ge(xused, e * XCH + (HI_E + j - RING_E + 1))
                    chunk_e(e, j)
            sp.wait_ge(y_out, 16 * NT)

        @block.tensor
        def _(pe):
            def ring_wait(c):
                pe.wait_ge(landed[PLAN[c][0]], 16 * PLAN[c][1])

            def xp_bank(i):
                if i >= 2:
                    pe.wait_ge(xp_taken, i - 1)
                return bank(6 + i % 2)

            pe.wait_ge(ident_ready, 1)
            for step in STEPS:
                kind = step[0]
                if kind == "vectors":
                    pe.wait_ge(small_in, 16 * N_SMALL)
                    b = xp_bank(transposes_before(step))
                    pe.transpose(b[:, 0:65], vrows[:, :], ident[0:65, 0:65]).then_inc(xp_done, 1)
                elif kind == "bmod":
                    b = xp_bank(transposes_before(step))
                    pe.transpose(b[:, 0:96], brows[:, :], ident[0:96, 0:96]).then_inc(xp_done, 1)
                elif kind == "cache":
                    b = xp_bank(transposes_before(step))
                    if step[1] == 0:
                        pe.wait_ge(cache_in, 32)
                    for h in range(4 if step[1] < 2 else 2):
                        src = cdk_rows[:, HD * (4 * step[1] + h):HD * (4 * step[1] + h + 1)] if step[1] < 2 \
                            else cgk_rows[:, HD * h:HD * (h + 1)]
                        mm = pe.transpose(b[:, HD * h:HD * (h + 1)], src, ident[:, :])
                    mm.then_inc(xp_done, 1)
                elif kind == "cols":
                    m = step[1]
                    pe.wait_ge(modA_act, m + 1)
                    if m == 0:
                        pe.wait_ge(modA_act, 2)
                        pe.wait_ge(modA_dve, 1)
                    b = xp_bank(transposes_before(step))
                    for k in range(KC):
                        mm = pe.transpose(b[:, 2 * k:2 * k + 2], mrowA[:, m, P * k:P * (k + 1)], ident[0:2, 0:2])
                    mm.then_inc(xp_done, 1)
                elif kind == "cols2":
                    pe.wait_ge(colrows_in, 64)
                    b = xp_bank(transposes_before(step))
                    pe.transpose(b[:, 0:64], colrows[:, :], ident[0:64, 0:64]).then_inc(xp_done, 1)
                elif kind == "sum":
                    m = step[1]
                    if m == 2:
                        pe.wait_ge(selv_ready, 2)
                    else:
                        pe.wait_ge(sum_taken, m - 2)
                    pe.wait_ge(mod_used, (m - 1) * KC)
                    for r in range(4):
                        for v in range(2):
                            mm = pe.matmul(bank(5)[32 * r:32 * (r + 1), :], selv[:, v, :], maccs[m][v][:, NB * r:NB * (r + 1)],
                                           start=(v == 0), stop=(v == 1), skip_group_check=True)
                    mm.then_inc(sum_done, 1)
                elif kind == "x":
                    k = step[1]
                    if k == 0:
                        pe.wait_ge(xn_ready, NT)
                    i = transposes_before(step)
                    b = xp_bank(i)
                    for t in range(TL):
                        mm = pe.transpose(b[:, P * t:P * (t + 1)], xrows[:, t, P * k:P * (k + 1)], ident[:, :])
                    mm.then_inc(xp_done, 1)
                    b = xp_bank(i + 1)
                    pe.transpose(b[:, 0:P], xrows[:, TL, P * k:P * (k + 1)], ident[:, :]).then_inc(xp_done, 1)
                elif kind == "modA":
                    _, m, k = step
                    if k == 0:
                        if m == 0:
                            pe.wait_ge(c_ready, 1)
                        else:
                            pe.wait_ge(xp_taken, 2)
                    ring_wait(step)
                    w = at(slot_b(step), 4, NB)
                    for c in range(4):
                        mm = pe.matmul(bank(4 * m + c)[0:2, :], cT[:, k, :], w[:, c, :], start=(k == 0), stop=(k == KC - 1))
                    if k < KC - 1:
                        mm.then_inc(used, 1)
                    else:
                        mm.then_inc(modA_done, 1)
                        pe.wait_ge(modA_done, m + 1)
                        pe.sem_inc(used, 1)
                elif kind == "projk":
                    _, blk, k = step
                    o = ORDER.index(blk)
                    n_k = KC * o + k
                    _, (x_hi, w_hi), (x_lo, w_lo) = split_b(n_k)
                    pe.wait_ge(pb_lo, n_k + 1)
                    if k == 0 and o == 0:
                        pe.wait_ge(modA_act, 2)
                    for t in range(NT):
                        if k == 0 and o > 0:
                            pe.wait_ge(proj_taken, NT * (o - 1) + t + 1)
                        ts = slice(P * t, P * (t + 1))
                        mm = three_products(pe, bank(t), (x_hi[:, ts], x_lo[:, ts]), (w_hi, w_lo), k == 0, k == KC - 1)
                        if k == KC - 1 and t < NT - 1:
                            mm.then_inc(proj_done, 1)
                    if k == KC - 1:
                        mm.then_inc(proj_done, 1)
                        pe.wait_ge(proj_done, NT * (o + 1))
                        pe.sem_inc(k_used, 1)
                    else:
                        mm.then_inc(k_used, 1)
                elif kind == "rows":
                    _, blk, t = step
                    b = xp_bank(transposes_before(step))
                    if (blk, t) in ROPED:
                        pe.wait_ge(roped, ROPED.index((blk, t)) + 1)
                    else:
                        pe.wait_ge(proj_taken, proj_count(blk, t))
                    for h in range(2 if blk == 8 else 4):
                        mm = pe.transpose(b[:, HD * h:HD * (h + 1)], prow[:, t, HD * h:HD * (h + 1)], ident[:, :])
                    mm.then_inc(xp_done, 1)

            def scores(u):
                t, j, comps, keys, kh, _ = unit(u)
                S = S_ps(u)
                k0 = 0 if t < TL else LAT + PAST
                if u >= 2:
                    pe.wait_ge(exp_done, u - 1)
                qs = slice(P * t, P * (t + 1))
                if comps == 1:
                    parts = [(0, 0, LAT), (0, LAT, keys)] if t < TL else [(0, 0, keys)]
                elif t < TL:
                    parts = [(0, LAT, keys), (1, 384, keys), (0, 0, LAT), (1, 0, 384)]
                else:
                    parts = [(0, 0, keys), (1, 0, keys)]
                for n, (c, lo, hi) in enumerate(parts):
                    if n == 3:
                        pe.wait_ge(tail_scored, diff_before(u + 1))
                    rows = slice(0, HD) if comps == 1 else slice(DQ * c, DQ * (c + 1))
                    mm = pe.matmul(S[:, TOK * c + lo:TOK * c + hi], qT[rows, j, qs], kT[rows, kh, k0 + lo:k0 + hi],
                                   start=True, stop=True, skip_group_check=True)
                    if n == 0 and len(parts) == 4:
                        mm.then_inc(tail_scored, 1)
                mm.then_inc(scored, 1)

            def prob_transposes(u):
                t, j, comps, keys, _, _ = unit(u)
                pe.wait_ge(probs_ready, u + 1)
                if not is_diff(u):
                    pe.wait_ge(exp_done, u + 1)
                if u >= 1:
                    pt_copied(pe, u - 1)
                n_ot = len([v for v in range(u) if ot_round(v)])
                if n_ot:
                    pe.wait_ge(ot_taken, n_ot)
                for b in range(min(4, keys // P)):
                    mm = pe.transpose(bank(6)[:, P * b:P * (b + 1)], E[:, u % 2, 0, P * b:P * (b + 1)], ident[:, :])
                if keys > 4 * P:
                    if u >= 1:
                        pe.wait_ge(o_taken, u)
                    mm = pe.transpose(bank(7)[:, 0:P], E[:, u % 2, 0, 4 * P:5 * P], ident[:, :])
                mm.then_inc(pt_done, 1)

            def values(u):
                t, j, comps, keys, kh, _ = unit(u)
                if u == 0:
                    pe.wait_ge(v_in, 96)
                pt_copied(pe, u)
                if u >= 1:
                    pe.wait_ge(o_taken, u)
                col = HD * kh
                nb = keys // P
                for b in range(nb):
                    mm = pe.matmul(bank(7)[:, P:2 * P], PT[:, u % 2, P * b:P * (b + 1)],
                                   V[:, b if t < TL else NT, col:col + HD], start=(b == 0), stop=(b == nb - 1))
                mm.then_inc(av_done, 1)

            def out_transposes(t, r):
                if r < 2:
                    pe.wait_ge(onorm_ready, t + 1)
                else:
                    pe.wait_ge(o_taken, HEADS * t + DH + 4 * (r - 2) + 4)
                for h in range(4):
                    mm = pe.transpose(bank(6)[:, HD * h:HD * (h + 1)], orow[:, 4 * r + h, :], ident[:, :])
                mm.then_inc(ot_done, 1)

            pe.wait_ge(xp_taken, XP_TOTAL)
            pe.wait_ge(proj_taken, NT * len(ORDER))
            pe.wait_ge(sum_taken, 4)
            scores(0)
            scores(1)
            for u in range(UNITS):
                prob_transposes(u)
                if u + 2 < UNITS:
                    scores(u + 2)
                values(u)
                if ot_round(u):
                    pt_copied(pe, u)
                    out_transposes(*ot_round(u))
            out_transposes(NT - 1, 2)
            pe.wait_ge(ot_taken, len(OT_LIST) - 1)
            out_transposes(NT - 1, 3)

            pe.wait_ge(ot_taken, len(OT_LIST))
            pe.wait_ge(exp_done, UNITS)

            def raw_transposes(n, t):
                i = NT * n + t
                pe.wait_ge(x1_done, i + 1)
                if i >= 2:
                    pe.wait_ge(rt_taken, i - 1)
                for c in range(4):
                    k = 4 * n + c
                    mm = pe.transpose(bank(5 + i % 2)[:, P * c:P * (c + 1)], x1[:, t, P * k:P * (k + 1)], ident[:, :])
                mm.then_inc(rt_done, 1)

            def router(n, t):
                i = NT * n + t
                pe.wait_ge(rt_taken, i + 1)
                for c in range(4):
                    k = 4 * n + c
                    mm = pe.matmul(bank(7)[:, NE * t:NE * (t + 1)], x1T[:, i % 2, P * c:P * (c + 1)],
                                   wrm[:, 0 if t < TL else 1, k, :], start=(i == 0 and c == 0), stop=(n == 3 and c == 3),
                                   skip_group_check=True)
                mm.then_inc(logits_done, 1)

            turn = []
            for n in range(4):
                for q in range(4):
                    i = 4 * n + q
                    _, w_hi, w_lo, _ = out_chunk(i)
                    pe.wait_ge(wo_lo, i + 1)
                    for j in range(4):
                        e = 4 * q + j
                        if n == 0:
                            pe.wait_ge(o_lo, e + 1)
                        for t in range(NT):
                            if e == 0 and n > 0:
                                pe.wait_ge(out_taken, NT * (n - 1) + t + 1)
                            ts, cs = slice(P * t, P * (t + 1)), slice(NB * j, NB * (j + 1))
                            mm = three_products(pe, bank(t), (oT_hi[e][:, ts], oT_lo[e][:, ts]), (w_hi[:, cs], w_lo[:, cs]),
                                                e == 0, e == HEADS - 1)
                            if e == HEADS - 1 and t < NT - 1:
                                mm.then_inc(out_done, 1)
                    if q < 3:
                        mm.then_inc(used, 1)
                    else:
                        mm.then_inc(out_done, 1)
                        pe.wait_ge(out_done, NT * (n + 1))
                        pe.sem_inc(used, 1)
                    if n > 0:
                        if n == 1 and q == 0:
                            pe.wait_ge(router_w, 2)
                        for t in ([q] if q < 3 else [3, 4]):
                            raw_transposes(n - 1, t)
                            turn.append((n - 1, t))
                            if len(turn) > 1:
                                router(*turn.pop(0))
            for t in range(NT):
                raw_transposes(3, t)
                turn.append((3, t))
                router(*turn.pop(0))
            while turn:
                router(*turn.pop(0))
            pe.wait_ge(out_taken, 4 * NT)
            for k in range(KC):
                mm = pe.matmul(bank(0)[0:2, 0:NE], modT[:, 3, :, k], wr[:, k, :], start=(k == 0), stop=(k == KC - 1))
            mm.then_inc(cst_done, 1)
            pe.wait_ge(cst_taken, 1)
            pe.wait_ge(sel_ready, 2)
            for v in range(2):
                mm = pe.matmul(bank(0)[:, NE * v:NE * (v + 1)], sel[:, v, :], cst[:, :], start=True, stop=True,
                               skip_group_check=True)
            mm.then_inc(cst_done, 1)
            pe.wait_ge(aff_ready, 1)
            for t in range(NT):
                mm = pe.transpose(bank(1 + t // 4)[0:NE, P * (t % 4):P * (t % 4 + 1)], aff[:, t, :], ident[:, :])
            mm.then_inc(affT_done, 1)
            pe.wait_ge(topk_ready, 1)
            pe.transpose(bank(3)[0:CAP, 0:NE], vals[:, :], ident[0:NE, 0:NE])
            pe.transpose(bank(3)[0:CAP, NE:2 * NE], idxf[:, :], ident[0:NE, 0:NE]).then_inc(cols_done, 1)
            pe.wait_ge(cols_ready, 1)

            def gathered_transposes():
                for k in range(KC):
                    mm = pe.transpose(bank(4 + k // 6)[:, CAP * (k % 6):CAP * (k % 6 + 1)],
                                      xs[0:CAP, P * k:P * (k + 1)], ident[0:CAP, 0:CAP])
                mm.then_inc(t1_done, 1)

            pe.sem_inc(xused, HI_E)
            pe.wait_ge(xs_ready, 1)
            gathered_transposes()
            with pe.Fori(0, NE) as e:
                def parts_wait(j):
                    pe.wait_ge(xw_lo, e * XCH + (j + 1))
                    pe.wait_ge(xw_lo2, e * XCH + (j + 1))

                pe.wait_ge(xsT_ready, e + 1)
                for part in range(2):
                    for j in range(8):
                        c = 8 * part + j
                        parts_wait(c)
                        w_hi, w_lo = split_e(c)
                        for i in range(2):
                            k = 2 * j + i
                            for h in range(2):
                                cs = slice(DE * i + NB * h, DE * i + NB * (h + 1))
                                mm = three_products(pe, bank(2 * part + h)[0:CAP, :], (xsT_hi[:, k, :], xsT_lo[:, k, :]),
                                                    (w_hi[:, cs], w_lo[:, cs]), k == 0, k == KC - 1)
                        mm.then_inc(xused, 1)
                    if part == 0:
                        pe.wait_ge(xs_ready, e + 2)
                        pe.wait_ge(rows_ready, e + 1)
                        gathered_transposes()
                for h in range(2):
                    pe.wait_ge(hid_half, e * 2 + (h + 1))
                    for f in range(4):
                        mm = pe.transpose(bank(h)[:, CAP * f:CAP * (f + 1)], sg[0:CAP, P * (4 * h + f):P * (4 * h + f + 1)],
                                          ident[0:CAP, 0:CAP])
                    mm.then_inc(ht_done, 1)
                pe.wait_ge(t1_scaled, e + 2)
                for f in range(8):
                    if f % 4 == 0:
                        pe.wait_ge(hidT_low, e * 2 + (f // 4 + 1))
                    parts_wait(16 + f)
                    w_hi, w_lo = split_e(16 + f)
                    for n in range(4):
                        cs = slice(NB * n, NB * (n + 1))
                        mm = three_products(pe, bank(4 + n)[0:CAP, :], (hidT_hi[:, f, :], hidT_lo[:, f, :]),
                                            (w_hi[:, cs], w_lo[:, cs]), f == 0, f == 7)
                    mm.then_inc(xused, 1)

        @block.scalar
        def _(act):
            for t in range(NT):
                act.dma_start(xrows[:, t, :], x_dram(t)).then_inc(x_in[t], 16)
            act.wait_ge(xp_taken, 1)
            act.activation(ctmp[:, :], vecT[:, 0:32], ACT.Exp, scale=-1.0).then_inc(silu_exp, 1)
            act.wait_ge(lam_sum, 1)
            act.activation(lame[:, :], lams[:, :], ACT.Exp).then_inc(lam_exp, 1)
            for t in range(NT):
                act.wait_ge(x_in[t], 16)
                if t > 0:
                    act.wait_ge(x_squared, t)
                act.activation(junkA, xrows[:, t, :], ACT.Square, accum_out=ssx[:, t:t + 1]).then_inc(x_squared, 1)

            for m in range(2):
                act.wait_ge(modA_done, m + 1)
                for c in range(4 if m == 0 else 2):
                    ins = act.activation(mrowA[:, m, NB * c:NB * (c + 1)], bank(4 * m + c)[0:2, :], ACT.Copy)
                ins.then_inc(modA_act, 1)

            def high_parts(n):
                (x, w), (x_hi, w_hi), _ = split_b(n)
                b, k = PK[n]
                if n < KC:
                    act.wait_ge(xp_taken, transposes_before(("x", k)) + 2)
                if n >= X_B:
                    act.wait_ge(k_used, n - X_B + 1)
                act.activation(x_hi, x, ACT.Copy)
                c = ("proj", b, k // 4)
                if k % 4 == 0:
                    act.wait_ge(landed[PLAN[c][0]], 16 * PLAN[c][1])
                act.activation(w_hi, w, ACT.Copy).then_inc(pb_hi, 1)

            def block_out(b):
                o = ORDER.index(b)
                former = [x for x in ORDER[:o] if x in ROWS_BLOCKS]
                keys = len([x for x in ORDER[:o] if x in KEY_BLOCKS])
                stored = len([x for x in ORDER[:o] if x in (8, 4)])
                if b == 5:
                    act.wait_ge(k_used, len(PK))
                    act.wait_ge(val_out, 16 * 2 * NT)
                    for cols, src in ((slice(DH * HD, VW), gv_d), (slice(0, NB), dv_d)):
                        act.dma_start(V[:, 0:TL, cols], src[0:LAT, :].rearrange("(t p) c -> p t c", p=P)).then_inc(v_in, 16)
                        act.dma_start(V[:, NT, cols], src[LAT:TOK, :]).then_inc(v_in, 16)
                    act.dma_start(V[:, TL, 0:DH * HD], cache_dv.rearrange("b o t h d -> (b o t) (h d)")).then_inc(v_in, 16)
                    act.dma_start(V[:, TL, DH * HD:VW], cache_gv.rearrange("b o t h d -> (b o t) (h d)")).then_inc(v_in, 16)
                for t in range(NT):
                    act.wait_ge(proj_done, NT * o + t + 1)
                    if b == 5:
                        act.activation(V[:, t if t < TL else NT, NB:2 * NB], bank(t), ACT.Copy).then_inc(proj_taken, 1)
                        continue
                    if former:
                        act.wait_ge(xp_done, transposes_before(("rows", former[-1], t)) + 1)
                        if t == TL and keys:
                            act.wait_ge(k_out, 16 * keys)
                        if stored:
                            act.wait_ge(val_out, 16 * (NT * stored))
                    act.activation(prow[:, t, :], bank(t), ACT.Copy).then_inc(proj_taken, 1)
                    if b in (8, 4):
                        act.wait_ge(proj_taken, NT * o + t + 1)
                        if b == 8:
                            act.dma_start(gv_d[P * t:P * (t + 1), :], prow[:, t, KVH * HD:]).then_inc(val_out, 16)
                        else:
                            act.dma_start(dv_d[P * t:P * (t + 1), :], prow[:, t, :]).then_inc(val_out, 16)

            def take(i):
                act.wait_ge(xp_done, i + 1)
                return bank(6 + i % 2)

            def modulated(k):
                i = transposes_before(("x", k))
                if k == 0:
                    act.wait_ge(xp_taken, i)
                for n, (v, cols) in enumerate(((0, slice(0, LAT)), (1, slice(LAT, TOK)))):
                    b = take(i + n)
                    act.activation(hT[:, k, cols], b[:, 0:cols.stop - cols.start], ACT.Identity,
                                   bias=modT[:, 0, v, k:k + 1], scale=A1[:, v, k:k + 1]).then_inc(xp_taken, 1)

            act.wait_ge(A1_ready, 1)
            n_k = 0
            for step in STEPS:
                if step[0] == "x":
                    modulated(step[1])
                    if step[1] < X_B - 1:
                        high_parts(step[1])
                elif step[0] == "rows":
                    _, blk, t = step
                    b = take(transposes_before(step))
                    if blk in (0, 1):
                        dst = qT[:, 4 * blk:4 * blk + 4, P * t:P * (t + 1)]
                    elif blk in (6, 7):
                        dst = qT[:, DH + 4 * (blk - 6):DH + 4 * (blk - 5), P * t:P * (t + 1)]
                    else:
                        col = P * t if t < TL else LAT + PAST
                        dst = kT[:, 4 * (blk - 2):4 * (blk - 1), col:col + P] if blk < 4 else kT[:, DH:DH + KVH, col:col + P]
                    h = dst.shape[1]
                    act.activation(dst, b[:, 0:h * HD].rearrange("p (h t) -> p h t", h=h), ACT.Copy).then_inc(xp_taken, 1)
                elif step[0] == "cache":
                    h0, n = ((0, 4), (4, 4), (8, 2))[step[1]]
                    b = take(transposes_before(step))
                    act.activation(kT[:, h0:h0 + n, LAT:LAT + PAST], b[:, 0:n * HD].rearrange("p (h t) -> p h t", h=n),
                                   ACT.Copy).then_inc(xp_taken, 1)
                elif step[0] == "cols2":
                    b = take(transposes_before(step))
                    act.activation(modT[:, 3:5], b[:, 0:64].rearrange("p (m v k) -> p m v k", m=2, v=2), ACT.Copy)\
                        .then_inc(xp_taken, 1)
                if step[0] == "projk":
                    n_k += 1
                    if n_k + X_B - 2 < len(PK):
                        high_parts(n_k + X_B - 2)
                if step[0] == "projk" and step[2] == KC - 1:
                    block_out(step[1])
                elif step[0] == "sum":
                    m = step[1]
                    act.wait_ge(sum_done, m - 1)
                    if m > 2:
                        act.wait_ge(mod_stored, 64 * (m - 2))
                    act.activation(mstage, bank(5), ACT.Copy).then_inc(sum_taken, 1)

            def exps(u):
                t, j, comps, keys, _, scale = unit(u)
                act.wait_ge(max_done, u + 1)
                if u >= 2:
                    act.wait_ge(pt_done, u - 1)
                for c in range(comps):
                    ins = act.activation(E[:, u % 2, c, 0:keys], S_ps(u)[:, TOK * c:TOK * c + keys], ACT.Exp,
                                         bias=nmax[:, u % 4, c:c + 1], scale=scale,
                                         accum_out=ssum[:, u % 4, c:c + 1])
                ins.then_inc(exp_done, 1)

            exps(0)
            exps(1)
            for u in range(UNITS):
                if is_diff(u):
                    keys = unit(u)[3]
                    act.wait_ge(pt_done, u + 1)
                    if u >= 2:
                        act.wait_ge(av_done, u - 1)
                    ins = act.activation(PT[:, u % 2, 0:min(keys, LAT)], bank(6)[:, 0:min(keys, LAT)], ACT.Copy)
                    if keys > LAT:
                        ins = act.activation(PT[:, u % 2, LAT:keys], bank(7)[:, 0:keys - LAT], ACT.Copy)
                    ins.then_inc(pt_act, 1)
                if u + 2 < UNITS:
                    exps(u + 2)

            act.wait_ge(av_done, UNITS)
            act.wait_ge(v_out, 32)
            act.wait_ge(mod_stored, 256)
            for t in range(NT):
                act.dma_start(x1[:, t, :], x_dram(t)).then_inc(x_again[t], 16)
            act.wait_ge(ot_taken, len(OT_LIST))
            act.dma_start(G1, mod_d[0].partition_broadcast(P)).then_inc(g1_in, 16)

            def high_out(i):
                raw, w_hi, _, c = out_chunk(i)
                act.wait_ge(landed[PLAN[c][0]], 16 * PLAN[c][1])
                if i >= HI_D:
                    act.wait_ge(used, OUT_USED + i - HI_D + 1)
                act.activation(w_hi[:, :], raw, ACT.Copy).then_inc(wo_hi, 1)

            def squares(n):
                for t in range(NT):
                    i = NT * n + t
                    act.wait_ge(x1_done, i + 1)
                    if i > 0:
                        act.wait_ge(x1_squared, i)
                    act.activation(junkD, x1[:, t, NB * n:NB * (n + 1)], ACT.Square,
                                   accum_out=ss2[:, t, n:n + 1]).then_inc(x1_squared, 1)

            high_out(0)
            for e in range(HEADS):
                act.activation(oT_hi[e][:, :], oT[:, e, :], ACT.Copy).then_inc(o_hi, 1)
            for i in range(1, 16):
                high_out(i)
                if i >= 6 and i % 4 == 2:
                    squares(i // 4 - 1)
            squares(3)
            act.wait_ge(rstd2_ready, 1)
            act.wait_ge(out_done, 4 * NT)
            for t in range(NT):
                act.activation(xn[:, t, :], x1[:, t, :], ACT.Copy, scale=rstd2[:, t:t + 1]).then_inc(xn2_ready, 1)
                if t == 0:
                    act.wait_ge(lshift_ready, 1)
                    act.activation(aff[:, :, :], logit[:, :, :], ACT.Exp).then_inc(lexp_done, 1)
                act.wait_ge(xn2_ready, t + 1)
                act.dma_start(xn_d[P * t:P * (t + 1), :], xn[:, t, :]).then_inc(xn_stored[t], 16)
            act.dma_start(G2[0:CL, :], mod_d[3, 0].partition_broadcast(CL)).then_inc(g2_in, 16)
            act.dma_start(G2[CL:CAP, :], mod_d[3, 1].partition_broadcast(CX)).then_inc(g2_in, 16)
            act.wait_ge(cols_ready, 1)
            act.dma_start(fgB, final_g.partition_broadcast(P)).then_inc(fg_in, 16)
            for t in range(NT):
                act.wait_ge(xn_stored[t], 16)
            with act.Fori(0, NE) as e:
                for j in range(XCH):
                    act.wait_ge(xlanded[j % RING_E], e * (16 * (XCH // RING_E)) + 16 * (j // RING_E + 1))
                    act.wait_ge(xused, e * XCH + (j + 1))
                    act.activation(split_e(j)[0][:, :], at(slot_e(j), D), ACT.Copy).then_inc(xw_hi, 1)
                    if j == 7 + HI_E:
                        act.wait_ge(xused, e * XCH + (HI_E + 8))
                        act.activation(sg[0:CAP, :], bank(0, 2)[0:CAP, :], ACT.Exp, scale=-1.0).then_inc(sig_exp, 1)
                    if j == 14 + HI_E:
                        for h in range(2):
                            act.wait_ge(ht_done, e * 2 + (h + 1))
                            act.activation(hidT_hi[:, 4 * h:4 * h + 4, :].rearrange("p f c -> p (f c)"),
                                           bank(h)[:, 0:4 * CAP], ACT.Copy).then_inc(hidT_half, 1)

            for t in range(NT):
                act.wait_ge(acc_in[t], 16)
                if t > 0:
                    act.wait_ge(f_squared, t)
                act.activation(junkF, x1[:, t, :], ACT.Square, accum_out=ssf[:, t:t + 1]).then_inc(f_squared, 1)
            for t in range(NT):
                act.wait_ge(y_ready, t + 1)
                dst = y_sample[0, P * t:P * (t + 1), :] if t < TL else y_prompt[0]
                act.dma_start(dst, x1[:, t, :]).then_inc(y_out, 16)
            act.wait_ge(y_out, 16 * NT)

        @block.gpsimd
        def _(pool):
            def rows16(v):
                return v.rearrange("o (k p) -> (o k) p", p=P)

            pool.dma_start(vrows[0:16, :], rows16(cvec)).then_inc(small_in, 16)
            pool.dma_start(vrows[16:32, :], c_ctx.rearrange("(k p) -> k p", p=P)).then_inc(small_in, 16)
            pool.dma_start(vrows[32:48, :], rows16(norm1_g)).then_inc(small_in, 16)
            pool.dma_start(vrows[48:64, :], rows16(norm2_g)).then_inc(small_in, 16)
            pool.dma_start(vrows[64:65, :], subln_g).then_inc(small_in, 16)
            pool.dma_start(brows[:, :], rows16(b_mod)).then_inc(small_in, 16)
            for i, v in enumerate((lq1, lq2, lk1, lk2)):
                pool.dma_start(lamv[:, i // 2, i % 2, :], v[0].partition_broadcast(P)).then_inc(small_in, 16)
            pool.dma_start(gains[:, 0, :], qn_g[0].partition_broadcast(P)).then_inc(small_in, 16)
            pool.dma_start(gains[:, 1, :], kn_g[0].partition_broadcast(P)).then_inc(small_in, 16)
            pool.memset(ident[:, :], 0.0).then_inc(ident_half, 1)
            pool.wait_ge(ident_half, 1)
            pool.affine_select(out=ident[:, :], in_=ident[:, :], compare_op=ALU.not_equal, fill=1.0, base=0,
                               pattern=[[-1, P]], channel_multiplier=1).then_inc(ident_ready, 1)
            pool.memset(mhalf[:, :], -0.5).then_inc(const_ready, 1)
            pool.memset(selv[:, :, :], 0.0).then_inc(selv_zero, 1)
            pool.wait_ge(selv_zero, 1)
            for v in range(2):
                pool.memset(selv[:, v, v:v + 1], 1.0).then_inc(selv_ready, 1)
            for v in range(2):
                pool.dma_start(mod_d[:, v, :], b_mod[0, 2 * D:].rearrange("(m n) -> m n", m=4)).then_inc(bias_in, 16)
            rope_v = rope.rearrange("(t p) c -> p t c", p=P)
            pool.dma_start(ropeD, rope_v[:, :, 0:2 * DQ].rearrange("p t (s d) -> p t s d", s=2)).then_inc(rope_in, 16)
            pool.dma_start(ropeQ, rope_v[:, :, 2 * DQ:].rearrange("p t (s d) -> p t s d", s=2)).then_inc(rope_in, 16)
            pool.dma_start(cdk_rows, cache_dk.rearrange("b o t h c d -> (b o t) (h c d)")).then_inc(cache_in, 16)
            pool.dma_start(cgk_rows, cache_gk.rearrange("b o t h d -> (b o t) (h d)")).then_inc(cache_in, 16)
            pool.wait_ge(const_ready, 1)

            def power(out, in_, n, done):
                exponent = mhalf[:, 0:n] if isinstance(n, int) else mhalf[:, 0:n[1]].unsqueeze(1).broadcast_to([P, *n])
                pool.tensor_tensor(out, in_, exponent, ALU.pow).then_inc(done, 1)

            pool.wait_ge(ms_ready, 1)
            power(rstd[:, :], ssx[:, :], NT, rstd_ready)
            def low_parts(n):
                (x, w), (x_hi, w_hi), (x_lo, w_lo) = split_b(n)
                pool.wait_ge(pb_hi, n + 1)
                pool.tensor_tensor(x_lo, x, x_hi.bitcast(F32), ALU.subtract)
                pool.tensor_tensor(w_lo, w, w_hi.bitcast(F32), ALU.subtract).then_inc(pb_lo, 1)

            for n in range(X_B - 1):
                low_parts(n)
            dk_v = new_dk.rearrange("b o t h c d -> (b o t) (h c d)")
            n_k = 0
            for step in STEPS:
                if step[0] == "sum":
                    m = step[1]
                    if m == 2:
                        pool.wait_ge(bias_in, 32)
                    pool.wait_ge(sum_taken, m - 1)
                    for r in range(4):
                        pool.dma_start(mod_d[m - 2, :, NB * r:NB * (r + 1)], mstage[32 * r:32 * r + 2, :],
                                       accum_op=ALU.add).then_inc(mod_stored, 16)
                if step[0] != "projk":
                    continue
                n_k += 1
                if n_k + X_B - 2 < len(PK):
                    low_parts(n_k + X_B - 2)
                if n_k == len(PK) - 12:
                    pool.wait_ge(mod_stored, 192)
                    for i in range(4):
                        pool.dma_start(colrows[16 * i:16 * (i + 1), :],
                                       mod_d[1 + i // 2, i % 2].rearrange("(k p) -> k p", p=P)).then_inc(colrows_in, 16)
                p, k = ORDER.index(step[1]), step[2]
                if p == 0:
                    continue
                b = ORDER[p - 1]
                if b >= 6 and k == 3:
                    h = 2 if b == 8 else 4
                    pool.wait_ge(rowms_ready, p)
                    power(rg[:, :, 0:h], ssg[:, :, 0:h], (NT, h), rowr_ready)
                if b in KEY_BLOCKS and k == 11:
                    if b == 8:
                        pool.wait_ge(roped, ROPED.index((8, TL)) + 1)
                        dst, src = new_gk.rearrange("b o t h d -> (b o t) (h d)"), prow[:, TL, 0:KVH * HD]
                    else:
                        pool.wait_ge(proj_taken, proj_count(b, TL))
                        dst, src = dk_v[:, (b - 2) * NB:(b - 1) * NB], prow[:, TL, :]
                    pool.dma_start(dst, src).then_inc(k_out, 16)
            pool.wait_ge(proj_taken, proj_count(5, TL))
            pool.wait_ge(v_in, 96)
            pool.dma_start(new_dv.rearrange("b o t h d -> (b o t) (h d)"), V[:, NT, 0:DH * HD]).then_inc(v_out, 16)
            pool.dma_start(new_gv.rearrange("b o t h d -> (b o t) (h d)"), V[:, NT, DH * HD:VW]).then_inc(v_out, 16)
            for t in range(NT):
                pool.wait_ge(oms_ready, t + 1)
                power(ro[:, :], sso[:, :], DH, or_ready)
            pool.wait_ge(ot_taken, len(OT_LIST))
            pool.dma_start(wr, w_router.rearrange("o (k p) e -> p (o k) e", p=P)).then_inc(wr_in, 16)
            pool.wait_ge(x1_done, 4 * NT)
            pool.dma_start(acc_d.rearrange("(t p) n -> p t n", p=P), x1).then_inc(acc_stored, 16)
            pool.wait_ge(ms2_ready, 1)
            power(rstd2[:, :], ms2[:, :], NT, rstd2_ready)

            pool.wait_ge(cols_ready, 1)
            pool.wait_ge(acc_stored, 16)
            for t in range(NT):
                pool.wait_ge(xn_stored[t], 16)

            def gather(e, upto):
                pool.tensor_copy(idxg[:, :], idxC[:, bass.ds(e, 1)]).then_inc(idx_set, 1)
                pool.wait_ge(idx_set, upto)
                pool.sem_inc(turn_taken, 1)
                pool.indirect_dma_start(xs[0:CAP, :], None, xn_d[:, :],
                                        bass.IndirectOffsetOnAxis(ap=idxg[:, 0:1], axis=0)).then_inc(gathered, 16)

            def scatter(e):
                pool.tensor_copy(idxs[:, :], idxC[:, bass.ds(e, 1)]).then_inc(idx_set, 1)
                pool.wait_ge(idx_set, e * 2 + 3)
                pool.wait_ge(rows_ready, e + 2)
                pool.sem_inc(turn_taken, 1)
                pool.indirect_dma_start(acc_d[:, :], bass.IndirectOffsetOnAxis(ap=idxs[:, 0:1], axis=0),
                                        xrow_out[0:CAP, :], None, compute_op=ALU.add).then_inc(scattered, 16)
                pool.wait_ge(scattered, e * 16 + 16)
                pool.sem_inc(row_free, 1)

            def low_tail(e, j):
                pool.wait_ge(xw_hi, e * XCH + (j + 1))
                w_hi, w_lo = split_e(j)
                pool.tensor_tensor(w_lo[:, SPLIT:], at(slot_e(j), D)[:, SPLIT:], w_hi[:, SPLIT:].bitcast(F32),
                                   ALU.subtract).then_inc(xw_lo2, 1)

            def expert_turn(e, last):
                for j in range(HI_E, XCH):
                    low_tail(e, j)
                    if j == HI_E:
                        pool.wait_ge(t1_done, e + 1)
                        gather(e + 1, e * 2 + 2)
                    if j == HI_E + 3:
                        pool.wait_ge(gathered, e * 16 + 32)
                        pool.sem_inc(xs_ready, 1)
                if not last:
                    for j in range(HI_E):
                        low_tail(e + 1, j)
                scatter(e)

            pool.sem_inc(row_free, 1)
            gather(0, 1)
            for j in range(HI_E):
                low_tail(0, j)
            pool.wait_ge(gathered, 16)
            pool.sem_inc(xs_ready, 1)
            with pool.Fori(0, NE - 1) as e:
                expert_turn(e, False)
            expert_turn(NE - 1, True)
            for t in range(NT):
                pool.dma_start(x1[:, t, :], acc_d[P * t:P * (t + 1), :]).then_inc(acc_in[t], 16)
            for t in range(NT):
                pool.wait_ge(fms_ready, t + 1)
                power(rf[:, t:t + 1], ssf[:, t:t + 1], 1, frstd_ready)

        @block.vector
        def _(dve):
            steps = [0]

            def link(ins):
                steps[0] += 1
                ins.then_inc(dve_step, 1)
                dve.wait_ge(dve_step, steps[0])

            def bc(v, n, axis=1):
                shape = list(v.shape)
                shape.insert(axis, n)
                return v.unsqueeze(axis).broadcast_to(shape)

            def take(i):
                dve.wait_ge(xp_done, i + 1)
                return bank(6 + i % 2)

            b = take(0)
            dve.tensor_copy(vecT[:, :], b[:, 0:65]).then_inc(xp_taken, 1)
            b = take(1)
            dve.tensor_copy(bmodT[:, :], b[:, 0:96]).then_inc(xp_taken, 1)
            link(dve.tensor_tensor(lamv[:, 0], lamv[:, 0], lamv[:, 1], ALU.mult))
            dve.tensor_reduce(lams[:, :], lamv[:, 0], AX, ALU.add).then_inc(lam_sum, 1)
            dve.wait_ge(silu_exp, 1)
            link(dve.tensor_scalar(ctmp[:, :], ctmp[:, :], 1.0, None, ALU.add))
            link(dve.reciprocal(ctmp[:, :], ctmp[:, :]))
            dve.tensor_tensor(cT.rearrange("p k v -> p v k"), vecT[:, 0:32].rearrange("p (v k) -> p v k", v=2),
                              ctmp[:, :].rearrange("p (v k) -> p v k", v=2), ALU.mult).then_inc(c_ready, 1)
            dve.wait_ge(lam_exp, 1)
            link(dve.tensor_tensor(neglam[:, :], lame[:, 1:2], lame[:, 0:1], ALU.subtract))
            link(dve.tensor_scalar(neglam[:, :], neglam[:, :], LAM_INIT, None, ALU.subtract))
            dve.wait_ge(rope_in, 32)
            for tab, g in ((ropeK, 1), (ropeQ, 0)):
                gn = gains[:, g, :]
                link(dve.tensor_tensor(tab[:, :, 0, :], ropeQ[:, :, 0, :], bc(gn, TL), ALU.mult))
                gsw = gn.rearrange("p (a h i) -> p a h i", a=2, h=2)
                for h in range(2):
                    for t in range(TL):
                        so = tab[:, t, 1, :].rearrange("p (a h i) -> p a h i", a=2, h=2)
                        si = ropeQ[:, t, 1, :].rearrange("p (a h i) -> p a h i", a=2, h=2)
                        link(dve.tensor_tensor(so[:, :, h, :], si[:, :, h, :], gsw[:, :, 1 - h, :], ALU.mult))
            dve.wait_ge(x_squared, NT)
            dve.tensor_scalar(ssx[:, :], ssx[:, :], 1.0 / D, EPS, ALU.mult, ALU.add).then_inc(ms_ready, 1)
            dve.wait_ge(rstd_ready, 1)
            for t in range(NT):
                dve.tensor_scalar(xrows[:, t, :], xrows[:, t, :], rstd[:, t:t + 1], None, ALU.mult).then_inc(xn_ready, 1)
            dve.wait_ge(modA_done, 2)
            for c in range(2, 4):
                ins = dve.tensor_copy(mrowA[:, 1, NB * c:NB * (c + 1)], bank(4 + c)[0:2, :])
            ins.then_inc(modA_dve, 1)

            def mean_squares(b):
                W, h = (KVH * HD, KVH) if b == 8 else (NB, NB // HD)
                for t in range(NT):
                    dve.wait_ge(proj_taken, proj_count(b, t))
                    if t == 0 and b != ORDER[0]:
                        dve.wait_ge(roped, len([r for r in ROPED if ORDER.index(r[0]) < ORDER.index(b)]))
                    v = prow[:, t, 0:W]
                    link(dve.tensor_tensor(rz[:, 0:W], v, v, ALU.mult))
                    ins = dve.tensor_reduce(ssg[:, t, 0:h], rz[:, 0:W].rearrange("p (h d) -> p h d", h=h), AX, ALU.add)
                    link(ins)
                dve.tensor_scalar(ssg[:, :, 0:h], ssg[:, :, 0:h], 1.0 / HD, EPS, ALU.mult, ALU.add).then_inc(rowms_ready, 1)

            def shape_rows(b, t):
                dve.wait_ge(proj_taken, proj_count(b, t))
                before = [r for r in ROPED if (ORDER.index(r[0]), r[1]) < (ORDER.index(b), t)]
                if before:
                    dve.wait_ge(roped, len(before))
                W = KVH * HD if b == 8 else NB
                v = prow[:, t, 0:W]
                if b >= 6:
                    h = W // HD
                    v3 = v.rearrange("p (h d) -> p h d", h=h)
                    if t == 0:
                        mean_squares(b)
                        dve.wait_ge(rowr_ready, ORDER.index(b) + 1)
                    link(dve.tensor_tensor(v3, v3, bc(rg[:, t, 0:h], HD, 2), ALU.mult))
                    if t == TL:
                        dve.tensor_tensor(v3, v3, bc(gains[:, 1 if b == 8 else 0, :], h), ALU.mult).then_inc(roped, 1)
                        return
                    tab, grp, q = (ropeK if b == 8 else ropeQ)[:, t], h, HD // 4
                else:
                    if t == TL:
                        return
                    tab, grp, q = ropeD[:, t], W // DQ, DQ // 4
                w = 4 * q
                y3, z3, vv = (x_[:, 0:W].rearrange("p (g d) -> p g d", d=w) for x_ in (ry, rz, prow[:, t]))
                dve.tensor_tensor(y3, vv, bc(tab[:, 0, :], grp), ALU.mult)
                for hf in range(2):
                    def half(x_, i):
                        return x_.rearrange("p (g a h i) -> p g a h i", a=2, h=2, i=q)[:, :, :, i, :]
                    s = tab[:, 1, :].rearrange("p (a h i) -> p a h i", a=2, h=2)[:, :, hf, :]
                    ins = dve.tensor_tensor(half(rz[:, 0:W], hf), half(v, 1 - hf), bc(s, grp), ALU.mult)
                link(ins)
                dve.tensor_tensor(v, ry[:, 0:W], rz[:, 0:W], ALU.add).then_inc(roped, 1)

            n_mod = n_rope = 0
            for step in STEPS:
                kind = step[0]
                if kind == "cols":
                    m = step[1]
                    b = take(transposes_before(step))
                    dve.tensor_tensor(modT[:, m], b[:, 0:32].rearrange("p (k v) -> p v k", v=2),
                                      bc(bmodT[:, KC * m:KC * (m + 1)], 2), ALU.add).then_inc(xp_taken, 1)
                    if m == 1:
                        dve.wait_ge(xp_taken, transposes_before(step) + 1)
                        dve.scalar_tensor_tensor(out=A1[:, :, :], in0=modT[:, 1], scalar=1.0, in1=bc(vecT[:, 32:48], 2),
                                                 op0=ALU.add, op1=ALU.mult).then_inc(A1_ready, 1)
                elif kind == "cols2":
                    dve.wait_ge(xp_taken, transposes_before(step) + 1)
                    link(dve.scalar_tensor_tensor(out=A2[:, :, :], in0=modT[:, 4], scalar=1.0,
                                                  in1=bc(vecT[:, 48:64], 2), op0=ALU.add, op1=ALU.mult))
                elif kind == "modB":
                    _, m, k = step
                    slot, fill, _ = PLAN[step]
                    dve.wait_ge(landed[slot], 16 * fill)
                    w = at(slot_b(step), D)
                    if k == 0:
                        if m > 2:
                            dve.wait_ge(sum_done, m - 2)
                        else:
                            dve.wait_ge(xp_done, transposes_before(("cols", 1)) + 1)
                    else:
                        dve.wait_ge(mod_used, n_mod)
                    for v in range(2):
                        if k == 0:
                            ins = dve.tensor_scalar(maccs[m][v], w, cT[:, k, v:v + 1], None, ALU.mult)
                        else:
                            ins = dve.scalar_tensor_tensor(out=maccs[m][v], in0=w, scalar=cT[:, k, v:v + 1],
                                                           in1=maccs[m][v], op0=ALU.mult, op1=ALU.add)
                    ins.then_inc(mod_used, 1)
                    n_mod += 1
                elif kind == "projk" and step[2] == KC - 1 and step[1] in ROWS_BLOCKS:
                    for t in range(NT):
                        shape_rows(step[1], t)

            def maxima(u):
                t, j, comps, keys, _, scale = unit(u)
                dve.wait_ge(scored, u + 1)
                if u >= 1:
                    dve.wait_ge(max_done, u)
                link(dve.tensor_reduce(mx[:, 0:comps],
                                       S_ps(u)[:, 0:2 * TOK].rearrange("p (c k) -> p c k", c=2)[:, 0:comps, 0:keys],
                                       AX, ALU.max))
                dve.tensor_scalar(nmax[:, u % 4, 0:comps], mx[:, 0:comps], -scale, None, ALU.mult).then_inc(max_done, 1)

            def combine(u):
                t, j, comps, keys, _, _ = unit(u)
                dve.wait_ge(exp_done, u + 1)
                if comps == 1:
                    dve.reciprocal(rsum[:, u % 4, 0:1], ssum[:, u % 4, 0:1]).then_inc(probs_ready, 1)
                    return
                if u >= 1:
                    dve.wait_ge(probs_ready, u)
                link(dve.reciprocal(rsum[:, u % 4, :], ssum[:, u % 4, :]))
                link(dve.scalar_tensor_tensor(out=coef[:, :], in0=ssum[:, u % 4, 0:1], scalar=neglam[:, 0:1],
                                              in1=rsum[:, u % 4, 1:2], op0=ALU.mult, op1=ALU.mult))
                dve.scalar_tensor_tensor(out=E[:, u % 2, 0, 0:keys], in0=E[:, u % 2, 1, 0:keys], scalar=coef[:, 0:1],
                                         in1=E[:, u % 2, 0, 0:keys], op0=ALU.mult, op1=ALU.add).then_inc(probs_ready, 1)

            def take_ot(t, r):
                dve.wait_ge(ot_done, OT_LIST.index((t, r)) + 1)
                dst = oT[:, 4 * r:4 * r + 4, P * t:P * (t + 1)]
                src = bank(6).rearrange("p (h t) -> p h t", h=4)
                if r < 2:
                    dve.tensor_scalar(dst, src, vecT[:, 64:65], 1.0 - LAM_INIT, ALU.mult, ALU.mult).then_inc(ot_taken, 1)
                else:
                    dve.tensor_copy(dst, src).then_inc(ot_taken, 1)

            dve.wait_ge(k_out, 48)
            dve.wait_ge(mod_stored, 256)
            dve.wait_ge(colrows_in, 64)
            maxima(0)
            maxima(1)
            combine(0)
            for u in range(UNITS):
                t, j, comps, keys, kh, _ = unit(u)
                if not is_diff(u):
                    dve.wait_ge(pt_done, u + 1)
                    if u >= 2:
                        dve.wait_ge(av_done, u - 1)
                    ins = dve.tensor_copy(PT[:, u % 2, 0:min(keys, LAT)], bank(6)[:, 0:min(keys, LAT)])
                    if keys > LAT:
                        ins = dve.tensor_copy(PT[:, u % 2, LAT:keys], bank(7)[:, 0:keys - LAT])
                    ins.then_inc(pt_dve, 1)
                if u + 1 < UNITS:
                    combine(u + 1)
                if u + 2 < UNITS:
                    maxima(u + 2)
                dve.wait_ge(av_done, u + 1)
                dve.tensor_scalar(orow[:, j, :], bank(7)[:, P:2 * P], rsum[:, u % 4, 0:1], None, ALU.mult)\
                    .then_inc(o_taken, 1)
                if j == DH - 1:
                    dve.wait_ge(o_taken, u + 1)
                    od = orow[:, 0:DH, :]
                    o3 = osq.rearrange("p (h d) -> p h d", h=DH)
                    link(dve.tensor_tensor(o3, od, od, ALU.mult))
                    link(dve.tensor_reduce(sso[:, :], o3, AX, ALU.add))
                    dve.tensor_scalar(sso[:, :], sso[:, :], 1.0 / HD, EPS, ALU.mult, ALU.add).then_inc(oms_ready, 1)
                if j == DH:
                    dve.wait_ge(or_ready, t + 1)
                    dve.tensor_tensor(orow[:, 0:DH, :], orow[:, 0:DH, :], bc(ro[:, :], HD, 2), ALU.mult)\
                        .then_inc(onorm_ready, 1)
                if ot_round(u):
                    take_ot(*ot_round(u))
            take_ot(NT - 1, 2)
            take_ot(NT - 1, 3)

            def take_raw(i):
                dve.wait_ge(rt_done, i + 1)
                if i >= 2:
                    dve.wait_ge(logits_done, i - 1)
                dve.tensor_copy(x1T[:, i % 2, :], bank(5 + i % 2)).then_inc(rt_taken, 1)

            def low_out(i):
                raw, w_hi, w_lo, _ = out_chunk(i)
                dve.wait_ge(wo_hi, i + 1)
                dve.tensor_tensor(w_lo[:, :], raw, w_hi[:, :].bitcast(F32), ALU.subtract).then_inc(wo_lo, 1)

            def residual(n):
                for t in range(NT):
                    i = NT * n + t
                    if n == 0:
                        dve.wait_ge(x_again[t], 16)
                    dve.wait_ge(out_done, i + 1)
                    v = 0 if t < TL else 1
                    cols = slice(NB * n, NB * (n + 1))
                    if i > 0:
                        dve.wait_ge(x1_done, i)
                    dve.tensor_tensor(gtmp, bank(t), G1[:, v, cols], ALU.mult).then_inc(out_taken, 1)
                    dve.wait_ge(out_taken, i + 1)
                    dve.tensor_tensor(x1[:, t, cols], x1[:, t, cols], gtmp, ALU.add).then_inc(x1_done, 1)

            low_out(0)
            for e in range(HEADS):
                dve.wait_ge(o_hi, e + 1)
                dve.tensor_tensor(oT_lo[e][:, :], oT[:, e, :], oT_hi[e][:, :].bitcast(F32), ALU.subtract).then_inc(o_lo, 1)
            low_out(1)
            dve.wait_ge(wr_in, 16)
            for v in range(2):
                dve.tensor_tensor(wrm[:, v], wr[:, :, :], bc(A2[:, v, :], NE, 2), ALU.mult).then_inc(router_w, 1)
            dve.wait_ge(g1_in, 16)
            for i in range(16):
                if i + 2 < 16:
                    low_out(i + 2)
                n, q = i // 4, i % 4
                if n > 0:
                    for t in ([q] if q < 3 else [3, 4]):
                        take_raw(NT * (n - 1) + t)
                if q == 3:
                    residual(n)
            for t in range(NT):
                take_raw(3 * NT + t)
            for v in range(2):
                dve.tensor_copy(sel[:, v, :], ident[0:2, v:v + 1].broadcast_to([2, P])).then_inc(sel_ready, 1)
            dve.wait_ge(cst_done, 1)
            dve.tensor_copy(cst[:, :], bank(0)[0:2, 0:NE]).then_inc(cst_taken, 1)
            dve.wait_ge(x1_squared, 4 * NT)
            link(dve.tensor_reduce(ms2[:, :], ss2[:, :, :], AX, ALU.add))
            dve.tensor_scalar(ms2[:, :], ms2[:, :], 1.0 / D, EPS, ALU.mult, ALU.add).then_inc(ms2_ready, 1)
            dve.wait_ge(cst_done, 2)
            link(dve.tensor_copy(cstB[:, :, :], bank(0)[:, 0:2 * NE].rearrange("p (v e) -> p v e", v=2)))
            dve.wait_ge(rstd2_ready, 1)
            dve.wait_ge(logits_done, 4 * NT)
            for t in range(NT):
                ins = dve.scalar_tensor_tensor(out=logit[:, t, :], in0=bank(7)[:, NE * t:NE * (t + 1)],
                                               scalar=rstd2[:, t:t + 1], in1=cstB[:, 0 if t < TL else 1, :],
                                               op0=ALU.mult, op1=ALU.add)
            link(ins)
            link(dve.tensor_reduce(lmax[:, :], logit[:, :, :], AX, ALU.max))
            dve.tensor_tensor(logit[:, :, :], logit[:, :, :], bc(lmax[:, :], NE, 2), ALU.subtract).then_inc(lshift_ready, 1)
            dve.wait_ge(lexp_done, 1)
            link(dve.tensor_reduce(lmax[:, :], aff[:, :, :], AX, ALU.add))
            link(dve.reciprocal(lmax[:, :], lmax[:, :]))
            dve.tensor_tensor(aff[:, :, :], aff[:, :, :], bc(lmax[:, :], NE, 2), ALU.mult).then_inc(aff_ready, 1)
            dve.wait_ge(affT_done, 1)
            link(dve.tensor_copy(affT[:, 0:LAT], bank(1)[0:NE, :]))
            link(dve.tensor_copy(affT[:, LAT:TOK], bank(2)[0:NE, 0:CTX]))
            for lo, hi, at0, count in ((0, LAT, 0, CL), (LAT, TOK, CL, CX)):
                row = affT[:, lo:hi]
                for r in range(count // 8):
                    top = slice(at0 + 8 * r, at0 + 8 * r + 8)
                    link(dve.max(vals[:, top], row))
                    link(dve.max_index(idx[:, top], vals[:, top], row))
                    if r < count // 8 - 1:
                        link(dve.match_replace(row, vals[:, top], row, -1.0))
            link(dve.tensor_copy(idxf[:, :], idx[:, :]))
            dve.tensor_scalar(idxf[:, CL:CAP], idxf[:, CL:CAP], float(LAT), None, ALU.add).then_inc(topk_ready, 1)
            dve.wait_ge(cols_done, 1)
            link(dve.tensor_copy(gateC[:, :], bank(3)[0:CAP, 0:NE]))
            link(dve.tensor_copy(idxC[:, 0:NE], bank(3)[0:CAP, NE:2 * NE]))
            dve.tensor_copy(idxC[:, NE:NE + 1], bank(3)[0:CAP, 2 * NE - 1:2 * NE]).then_inc(cols_ready, 1)
            for t in range(NT):
                dve.wait_ge(xn_stored[t], 16)

            lat, con = slice(0, CL), slice(CL, CAP)
            kinds = ((0, lat), (1, con))
            groups = [(g, min(6, KC - 6 * g)) for g in range(3)]

            def scale_rows():
                for g, n in groups:
                    src = bank(4 + g)[:, 0:n * CAP].rearrange("p (k c) -> p k c", k=n)
                    for v, cs in kinds:
                        ins = dve.tensor_tensor(xstage[:, 6 * g:6 * g + n, cs], src[:, :, cs],
                                                bc(A2[:, v, 6 * g:6 * g + n], cs.stop - cs.start, 2), ALU.mult)
                ins.then_inc(t1_scaled, 1)

            def shift_rows(n):
                for v, cs in kinds:
                    ins = dve.tensor_tensor(xstage[:, :, cs], xstage[:, :, cs], bc(modT[:, 3, v, :], cs.stop - cs.start, 2),
                                            ALU.add)
                ins.then_inc(xsum_ready, 1)
                dve.wait_ge(xsum_ready, n)
                dve.tensor_copy(xsT_hi, xstage).then_inc(xhi_ready, 1)
                dve.wait_ge(xhi_ready, n)
                dve.tensor_tensor(xsT_lo, xstage, xsT_hi.bitcast(F32), ALU.subtract).then_inc(xsT_ready, 1)

            def low_part(e, j):
                dve.wait_ge(xw_hi, e * XCH + (j + 1))
                w_hi, w_lo = split_e(j)
                dve.tensor_tensor(w_lo[:, 0:SPLIT], at(slot_e(j), D)[:, 0:SPLIT], w_hi[:, 0:SPLIT].bitcast(F32),
                                  ALU.subtract).then_inc(xw_lo, 1)

            def reciprocal(h, n):
                cs = slice(NB * h, NB * (h + 1))
                dve.wait_ge(sig_add, n)
                dve.reciprocal(sg[0:CAP, cs], sg[0:CAP, cs]).then_inc(sig_rec, 1)

            def hidden_low(h, n):
                dve.wait_ge(hidT_half, n)
                dve.tensor_tensor(hidT_lo[:, 4 * h:4 * h + 4, :].rearrange("p f c -> p (f c)"), bank(h)[:, 0:4 * CAP],
                                  hidT_hi[:, 4 * h:4 * h + 4, :].rearrange("p f c -> p (f c)").bitcast(F32),
                                  ALU.subtract).then_inc(hidT_low, 1)

            def expert_turn(e, last):
                for j in range(HI_E - 1, XCH):
                    low_part(e, j)
                    if j == 11:
                        dve.wait_ge(sig_exp, e + 1)
                        dve.tensor_scalar(sg[0:CAP, :], sg[0:CAP, :], 1.0, None, ALU.add).then_inc(sig_add, 1)
                        reciprocal(0, e + 1)
                    if j == 12:
                        reciprocal(1, e + 1)
                    if j == 13:
                        dve.wait_ge(sig_rec, e * 2 + 2)
                        dve.tensor_tensor(sg[0:CAP, :], bank(0, 2)[0:CAP, :], sg[0:CAP, :], ALU.mult).then_inc(sig_mul, 1)
                    if j == 14:
                        dve.wait_ge(t1_done, e + 2)
                        dve.wait_ge(xsT_ready, e + 1)
                        scale_rows()
                    if j == 14 + HI_E:
                        dve.wait_ge(sig_mul, e + 1)
                        dve.wait_ge(xused, e * XCH + (HI_E + 16))
                        for h in range(2):
                            cs = slice(NB * h, NB * (h + 1))
                            dve.tensor_tensor(sg[0:CAP, cs], bank(2 + h)[0:CAP, :], sg[0:CAP, cs], ALU.mult)\
                                .then_inc(hid_half, 1)
                        for h in range(2):
                            hidden_low(h, e * 2 + (h + 1))
                    if j == 16 + HI_E:
                        dve.wait_ge(t1_scaled, e + 2)
                        shift_rows(e + 2)
                    if j == 18 + HI_E:
                        dve.wait_ge(rows_ready, e + 1)
                        dve.tensor_copy(gcol[:, :], gateC[:, bass.ds(e, 1)]).then_inc(gcol_ready, 1)
                if not last:
                    for j in range(HI_E - 1):
                        low_part(e + 1, j)
                dve.wait_ge(gcol_ready, e + 1)
                dve.wait_ge(row_free, e + 1)
                dve.wait_ge(xused, e * XCH + (HI_E + 24))
                for n in range(4):
                    cs = slice(NB * n, NB * (n + 1))
                    ins = dve.scalar_tensor_tensor(out=xrow_out[0:CAP, cs], in0=bank(4 + n)[0:CAP, :], scalar=gcol[:, 0:1],
                                                   in1=G2[0:CAP, cs], op0=ALU.mult, op1=ALU.mult)
                ins.then_inc(rows_ready, 1)

            dve.sem_inc(rows_ready, 1)
            for j in range(HI_E - 1):
                low_part(0, j)
            dve.wait_ge(t1_done, 1)
            scale_rows()
            dve.wait_ge(t1_scaled, 1)
            shift_rows(1)
            dve.wait_ge(g2_in, 32)
            with dve.Fori(0, NE - 1) as e:
                expert_turn(e, False)
            expert_turn(NE - 1, True)

            dve.wait_ge(fg_in, 16)
            for t in range(NT):
                dve.wait_ge(f_squared, t + 1)
                dve.tensor_scalar(ssf[:, t:t + 1], ssf[:, t:t + 1], 1.0 / D, EPS, ALU.mult, ALU.add).then_inc(fms_ready, 1)
                dve.wait_ge(frstd_ready, t + 1)
                dve.scalar_tensor_tensor(out=x1[:, t, :], in0=x1[:, t, :], scalar=rf[:, t:t + 1], in1=fgB,
                                         op0=ALU.mult, op1=ALU.mult).then_inc(y_ready, 1)


def rope_tables():
    t = np.arange(LAT)
    row, col = (t // GRID_W).astype(np.float32), (t % GRID_W).astype(np.float32)
    cols = []
    for dim in (DQ, HD):
        sec = dim // 2
        inv = (10000.0 ** (-np.arange(0, sec, 2, dtype=np.float32) / sec)).astype(np.float32)
        ang = np.stack([row[:, None] * inv, col[:, None] * inv], axis=1)
        sign = np.array([-1.0, 1.0], np.float32)[None, None, :, None]
        both = np.stack([ang, ang], axis=2)
        cols += [np.cos(both).reshape(LAT, dim), (np.sin(both) * sign).reshape(LAT, dim)]
    return np.concatenate(cols, axis=1).astype(np.float32)


_INS = ["x_prompt", "x_sample", "c", "cache_diff_k", "cache_diff_v", "cache_gqa_k", "cache_gqa_v", "c_ctx",
        "norm1_g", "norm2_g", "w_mod", "b_mod", "w_in", "w_out", "diff_lambda_q1", "diff_lambda_k1",
        "diff_lambda_q2", "diff_lambda_k2", "diff_subln_g", "gqa_q_norm_g", "gqa_k_norm_g", "w_router",
        "w_expert_gate", "w_expert_up", "w_expert_down", "final_norm_g"]
_OUTS = [(1, CTX, D), (1, LAT, D), (1, 1, CTX, DH, 2, DQ), (1, 1, CTX, DH, HD), (1, 1, CTX, KVH, HD),
         (1, 1, CTX, KVH, HD)]


def kernel(**inputs):
    import concourse.bacc as _bacc
    from concourse.bass_utils import run_bass_kernel_spmd as _run

    nc = _bacc.Bacc("TRN2", target_bir_lowering=False, num_devices=1)
    arrays, args = {}, []
    for name in _INS:
        v = np.ascontiguousarray(inputs[name])
        arrays[f"in_{name}"] = v
        args.append(nc.dram_tensor(f"in_{name}", v.shape, F32, kind="ExternalInput").ap())
    arrays["in_rope"] = rope_tables()
    rope = nc.dram_tensor("in_rope", arrays["in_rope"].shape, F32, kind="ExternalInput").ap()
    outs = [nc.dram_tensor(f"out_{i}", s, F32, kind="ExternalOutput").ap() for i, s in enumerate(_OUTS)]
    build(nc, args, rope, outs)
    r = _run(nc, [arrays], core_ids=[0])
    return tuple(r.results[0][f"out_{i}"] for i in range(len(_OUTS)))
```
